# Optimizing a Trainium2 kernel written in Bass

```python
import jax, jax.numpy as jnp
from jax import lax
import numpy as np

D_MODEL = 1024
BATCH = 1
SEQ = 2048
DEPTH = 1
DEC_BATCH = 1
DEC_SEQ = 64
PAST_LEN = 512

CHUNK = 64
QBLOCK = 128
HEAD_DIM = 64
N_HEADS = (D_MODEL // 2) // HEAD_DIM
N_KV_HEADS = 2
IDX_HEADS = 8
IDX_DIM = 32
TOPK_MAX = 256
MEM_TOKENS = 256
MEM_HEADS = 4
MEM_WIDTH = MEM_HEADS * HEAD_DIM
POOL_WIDTH = D_MODEL // 4
POOL_GROUPS = 4
POOL_WINDOWS = (2, 4, 8, 16)
POOL_HIST = 15
ATTN_WIDTH = N_HEADS * HEAD_DIM
MIX_WIDTH = POOL_WIDTH + ATTN_WIDTH + MEM_WIDTH
D_FF = 2816
CONV_W = 3
ROPE_THETA = 500000.0
ROT_DIM = HEAD_DIM // 4
IDX_ROT_DIM = IDX_DIM // 4
EPS = 1e-6
SPLITS = (POOL_WIDTH, N_HEADS * HEAD_DIM, N_KV_HEADS * HEAD_DIM, N_KV_HEADS * HEAD_DIM,
          IDX_HEADS * IDX_DIM, IDX_DIM, IDX_HEADS, MEM_WIDTH)
IN_WIDTH = sum(SPLITS)

kernel_name = "hybrid_pool_dsa_memory_streaming_step"

def rms_norm(x, g):
    xf = x.astype(jnp.float32)
    y = xf * lax.rsqrt(jnp.mean(xf * xf, axis=-1, keepdims=True) + EPS)
    return (y * g.astype(jnp.float32)).astype(x.dtype)

def partial_rope(x, pos, rot_dim):
    half = rot_dim // 2
    inv = ROPE_THETA ** (-jnp.arange(half, dtype=jnp.float32) / half)
    ang = pos.astype(jnp.float32)[:, None] * inv[None, :]
    cos = jnp.cos(ang)[:, None, :]
    sin = jnp.sin(ang)[:, None, :]
    xr = x[..., :rot_dim].astype(jnp.float32)
    x1, x2 = xr[..., :half], xr[..., half:]
    rot = jnp.concatenate([x1 * cos - x2 * sin, x2 * cos + x1 * sin], axis=-1)
    return jnp.concatenate([rot.astype(x.dtype), x[..., rot_dim:]], axis=-1)

def project(x, pos, lw):
    B, T, _ = x.shape
    n = rms_norm(x, lw['norm1'])
    proj = n @ lw['w_in']
    cuts = [int(c) for c in np.cumsum(SPLITS)[:-1]]
    u, q, k, v, qi, ki, wi, qm = jnp.split(proj, cuts, axis=-1)
    q = partial_rope(rms_norm(q.reshape(B, T, N_HEADS, HEAD_DIM), lw['q_norm']), pos, ROT_DIM)
    k = partial_rope(rms_norm(k.reshape(B, T, N_KV_HEADS, HEAD_DIM), lw['k_norm']), pos, ROT_DIM)
    v = v.reshape(B, T, N_KV_HEADS, HEAD_DIM)
    qi = partial_rope(qi.reshape(B, T, IDX_HEADS, IDX_DIM), pos, IDX_ROT_DIM) * (IDX_DIM ** -0.5)
    ki = partial_rope(ki.reshape(B, T, 1, IDX_DIM), pos, IDX_ROT_DIM)[:, :, 0]
    wi = wi * (IDX_HEADS ** -0.5)
    qm = rms_norm(qm.reshape(B, T, MEM_HEADS, HEAD_DIM), lw['mem_q_norm'])
    return u, q, k, v, qi, ki, wi, qm

def pool_mixer(u, hist, pos0, lw):
    B, T, W = u.shape
    ext = jnp.concatenate([hist, u], axis=1)
    extf = ext.astype(jnp.float32)
    cs = jnp.concatenate([jnp.zeros((B, 1, W), jnp.float32), jnp.cumsum(extf, axis=1)], axis=1)
    pos = pos0 + jnp.arange(T)
    gw = W // POOL_GROUPS
    means = []
    for g, w in enumerate(POOL_WINDOWS):
        c0, c1 = g * gw, (g + 1) * gw
        s = cs[:, POOL_HIST + 1:POOL_HIST + 1 + T, c0:c1] - cs[:, POOL_HIST + 1 - w:POOL_HIST + 1 - w + T, c0:c1]
        cnt = jnp.minimum(w, pos + 1).astype(jnp.float32)[None, :, None]
        means.append(s / cnt)
    z = (jnp.concatenate(means, axis=-1) - u.astype(jnp.float32)).reshape(B, T, POOL_GROUPS, gw)
    y = jnp.einsum('btgc,gcd->btgd', z, lw['pool_w'].astype(jnp.float32)).reshape(B, T, W)
    y = y * lw['pool_scale'].astype(jnp.float32)
    return y.astype(u.dtype), ext[:, -POOL_HIST:]

def dsa_block(q, qi, wi, limit, k, v, ki, top_k):
    B, T = q.shape[0], q.shape[1]
    L = k.shape[1]
    s = jnp.einsum('bthd,bsd->bths', qi.astype(jnp.float32), ki.astype(jnp.float32))
    score = jnp.einsum('bth,bths->bts', wi.astype(jnp.float32), jax.nn.relu(s))
    visible = jnp.arange(L)[None, :] < limit[:, None]
    score = jnp.where(visible[None], score, -jnp.inf)
    top_val, top_idx = lax.top_k(score, top_k)
    valid = jnp.isfinite(top_val)
    take = jax.vmap(lambda rows, idx: rows[idx])
    k_sel = take(k, top_idx).astype(jnp.float32)
    v_sel = take(v, top_idx).astype(jnp.float32)
    qg = q.reshape(B, T, N_KV_HEADS, N_HEADS // N_KV_HEADS, HEAD_DIM).astype(jnp.float32)
    logits = jnp.einsum('btjgd,btnjd->btjgn', qg, k_sel) * (HEAD_DIM ** -0.5)
    logits = jnp.where(valid[:, :, None, None, :], logits, -jnp.inf)
    p = jax.nn.softmax(logits, axis=-1)
    o = jnp.einsum('btjgn,btnjd->btjgd', p, v_sel)
    return o.reshape(B, T, N_HEADS * HEAD_DIM).astype(q.dtype)

def dsa_prompt(q, qi, wi, k, v, ki, top_k):
    B, S = q.shape[0], q.shape[1]
    nb = S // QBLOCK
    def blocks(a):
        return jnp.swapaxes(a.reshape((B, nb, QBLOCK) + a.shape[2:]), 0, 1)
    limit = ((jnp.arange(S) // CHUNK + 1) * CHUNK).reshape(nb, QBLOCK)
    out = lax.map(lambda a: dsa_block(a[0], a[1], a[2], a[3], k, v, ki, top_k),
                  (blocks(q), blocks(qi), blocks(wi), limit))
    return jnp.swapaxes(out, 0, 1).reshape(B, S, N_HEADS * HEAD_DIM)

def memory_kv(mem, lw):
    B, M, _ = mem.shape
    m = rms_norm(mem, lw['mem_norm'])
    mk = rms_norm((m @ lw['w_mem_k']).reshape(B, M, MEM_HEADS, HEAD_DIM), lw['mem_k_norm'])
    mv = (m @ lw['w_mem_v']).reshape(B, M, MEM_HEADS, HEAD_DIM)
    return mk, mv

def mem_attend(qm, mk, mv):
    B, T = qm.shape[0], qm.shape[1]
    logits = jnp.einsum('bthd,bmhd->bhtm', qm.astype(jnp.float32), mk.astype(jnp.float32)) * (HEAD_DIM ** -0.5)
    p = jax.nn.softmax(logits, axis=-1)
    o = jnp.einsum('bhtm,bmhd->bthd', p, mv.astype(jnp.float32))
    return o.reshape(B, T, MEM_WIDTH).astype(qm.dtype)

def out_and_ffn(x, a_pool, a_attn, a_mem, conv_hist, lw):
    h = x + jnp.concatenate([a_pool, a_attn, a_mem], axis=-1) @ lw['w_out']
    n = rms_norm(h, lw['norm2'])
    up = n @ lw['w_up']
    T = up.shape[1]
    ext = jnp.concatenate([conv_hist, up], axis=1)
    c = lw['conv_b']
    for j in range(CONV_W):
        c = c + ext[:, j:j + T] * lw['conv_w'][j]
    g, val = jnp.split(c, 2, axis=-1)
    y = h + (jax.nn.silu(g) * val) @ lw['w_down']
    return y, ext[:, -(CONV_W - 1):]

def prompt_layer(x, mem, lw):
    B, S, _ = x.shape
    pos = jnp.arange(S)
    u, q, k, v, qi, ki, wi, qm = project(x, pos, lw)
    a_pool, pool_state = pool_mixer(u, jnp.zeros((B, POOL_HIST, POOL_WIDTH), x.dtype), 0, lw)
    a_attn = dsa_prompt(q, qi, wi, k, v, ki, min(TOPK_MAX, S // 4))
    mk, mv = memory_kv(mem, lw)
    a_mem = mem_attend(qm, mk, mv)
    y, conv_state = out_and_ffn(x, a_pool, a_attn, a_mem,
                                jnp.zeros((B, CONV_W - 1, 2 * D_FF), x.dtype), lw)
    return y, (k, v, ki, mk, mv, pool_state, conv_state)

def sample_layer(x, ck, cv, cki, cmk, cmv, cpool, cconv, lw):
    B, T, _ = x.shape
    P = ck.shape[1]
    pos = P + jnp.arange(T)
    u, q, k, v, qi, ki, wi, qm = project(x, pos, lw)
    a_pool, pool_state = pool_mixer(u, cpool, P, lw)
    L = P + T
    k_all = jnp.concatenate([ck, k], axis=1)
    v_all = jnp.concatenate([cv, v], axis=1)
    ki_all = jnp.concatenate([cki, ki], axis=1)
    a_attn = dsa_block(q, qi, wi, jnp.full((T,), L, jnp.int32), k_all, v_all, ki_all, min(TOPK_MAX, L // 4))
    a_mem = mem_attend(qm, cmk, cmv)
    y, conv_state = out_and_ffn(x, a_pool, a_attn, a_mem, cconv, lw)
    return y, (k, v, ki, pool_state, conv_state)

def setup_inputs(seed: int = 0) -> dict:
    key = jax.random.key(seed)
    ks = jax.random.split(key, 32)
    f32 = jnp.float32
    def nrm(k, shape, scale=1.0):
        return jax.random.normal(k, shape, f32) * scale
    def gain(k, shape):
        return 1.0 + 0.02 * jax.random.normal(k, shape, f32)
    gw = POOL_WIDTH // POOL_GROUPS
    return {
        "x_prompt": nrm(ks[0], (BATCH, SEQ, D_MODEL)),
        "x_sample": nrm(ks[1], (DEC_BATCH, DEC_SEQ, D_MODEL)),
        "mem_prompt": nrm(ks[2], (BATCH, MEM_TOKENS, D_MODEL)),
        "cache_k": nrm(ks[3], (DEPTH, DEC_BATCH, PAST_LEN, N_KV_HEADS, HEAD_DIM)),
        "cache_v": nrm(ks[4], (DEPTH, DEC_BATCH, PAST_LEN, N_KV_HEADS, HEAD_DIM)),
        "cache_kidx": nrm(ks[5], (DEPTH, DEC_BATCH, PAST_LEN, IDX_DIM)),
        "cache_mem_k": nrm(ks[6], (DEPTH, DEC_BATCH, MEM_TOKENS, MEM_HEADS, HEAD_DIM)),
        "cache_mem_v": nrm(ks[7], (DEPTH, DEC_BATCH, MEM_TOKENS, MEM_HEADS, HEAD_DIM)),
        "state_pool": nrm(ks[8], (DEPTH, DEC_BATCH, POOL_HIST, POOL_WIDTH)),
        "state_ffn_conv": nrm(ks[9], (DEPTH, DEC_BATCH, CONV_W - 1, 2 * D_FF)),
        "norm1": gain(ks[10], (DEPTH, D_MODEL)),
        "w_in": nrm(ks[11], (DEPTH, D_MODEL, IN_WIDTH), D_MODEL ** -0.5),
        "q_norm": gain(ks[12], (DEPTH, HEAD_DIM)),
        "k_norm": gain(ks[13], (DEPTH, HEAD_DIM)),
        "pool_w": nrm(ks[14], (DEPTH, POOL_GROUPS, gw, gw), gw ** -0.5),
        "pool_scale": 1.0 + 0.1 * jax.random.normal(ks[15], (DEPTH, POOL_WIDTH), f32),
        "mem_norm": gain(ks[16], (DEPTH, D_MODEL)),
        "w_mem_k": nrm(ks[17], (DEPTH, D_MODEL, MEM_WIDTH), D_MODEL ** -0.5),
        "w_mem_v": nrm(ks[18], (DEPTH, D_MODEL, MEM_WIDTH), D_MODEL ** -0.5),
        "mem_q_norm": gain(ks[19], (DEPTH, HEAD_DIM)),
        "mem_k_norm": gain(ks[20], (DEPTH, HEAD_DIM)),
        "w_out": nrm(ks[21], (DEPTH, MIX_WIDTH, D_MODEL), MIX_WIDTH ** -0.5),
        "norm2": gain(ks[22], (DEPTH, D_MODEL)),
        "w_up": nrm(ks[23], (DEPTH, D_MODEL, 2 * D_FF), D_MODEL ** -0.5),
        "conv_w": nrm(ks[24], (DEPTH, CONV_W, 2 * D_FF), CONV_W ** -0.5),
        "conv_b": nrm(ks[25], (DEPTH, 2 * D_FF), 0.01),
        "w_down": nrm(ks[26], (DEPTH, D_FF, D_MODEL), D_FF ** -0.5),
    }

def reference(x_prompt, x_sample, mem_prompt, cache_k, cache_v, cache_kidx, cache_mem_k, cache_mem_v,
              state_pool, state_ffn_conv, norm1, w_in, q_norm, k_norm, pool_w, pool_scale, mem_norm,
              w_mem_k, w_mem_v, mem_q_norm, mem_k_norm, w_out, norm2, w_up, conv_w, conv_b, w_down):
    xp = x_prompt
    xs = x_sample
    p_states = []
    s_states = []
    for l in range(DEPTH):
        lw = {'norm1': norm1[l], 'w_in': w_in[l], 'q_norm': q_norm[l], 'k_norm': k_norm[l],
              'pool_w': pool_w[l], 'pool_scale': pool_scale[l], 'mem_norm': mem_norm[l],
              'w_mem_k': w_mem_k[l], 'w_mem_v': w_mem_v[l], 'mem_q_norm': mem_q_norm[l],
              'mem_k_norm': mem_k_norm[l], 'w_out': w_out[l], 'norm2': norm2[l], 'w_up': w_up[l],
              'conv_w': conv_w[l], 'conv_b': conv_b[l], 'w_down': w_down[l]}
        xp, st_p = prompt_layer(xp, mem_prompt, lw)
        p_states.append(st_p)
        xs, st_s = sample_layer(xs, cache_k[l], cache_v[l], cache_kidx[l], cache_mem_k[l], cache_mem_v[l],
                                state_pool[l], state_ffn_conv[l], lw)
        s_states.append(st_s)
    k_p, v_p, kidx_p, memk_p, memv_p, pool_p, conv_p = [jnp.stack(z) for z in zip(*p_states)]
    k_s, v_s, kidx_s, pool_s, conv_s = [jnp.stack(z) for z in zip(*s_states)]
    return (xp, xs, k_p, v_p, kidx_p, memk_p, memv_p, pool_p, conv_p, k_s, v_s, kidx_s, pool_s, conv_s)


_drawn_inputs = setup_inputs


def setup_inputs(seed=0):
    import zlib

    import numpy as np

    out = dict(_drawn_inputs(seed))
    spreads = {}
    factors = {'norm1': 2.824,
     'q_norm': 8.0,
     'k_norm': 2.813,
     'mem_norm': 2.847,
     'mem_q_norm': 8.0,
     'mem_k_norm': 2.954,
     'norm2': 2.816,
     'conv_b': 8.0,
     'state_pool': 2.867}
    for name, (base, spread) in spreads.items():
        noise = np.random.default_rng([zlib.crc32(name.encode()), seed]).standard_normal(out[name].shape)
        drawn = base * np.exp(spread * noise) if base else spread * noise
        out[name] = __import__('jax').numpy.asarray(drawn.astype(out[name].dtype))
    for name, factor in factors.items():
        out[name] = (out[name] * factor).astype(out[name].dtype)
    return out
```

```python
import numpy as np
from contextlib import ExitStack

import concourse.bass as bass
import concourse.mybir as mybir
from concourse.alu_op_type import AluOpType as ALU

F32, F32R, I32 = mybir.dt.float32, mybir.dt.float32r, mybir.dt.int32
ACT = mybir.ActivationFunctionType
AX = mybir.AxisListType

P = 128
D, SEQ, TS, PAST = 1024, 2048, 64, 512
ROWS = SEQ + TS
KC = D // P
NB = SEQ // P
HD, NH, NKV = 64, 8, 2
GQ = NH // NKV
IH, ID = 8, 32
MT, MH = 256, 4
PW, PG, HIST = 256, 4, 15
WINDOWS = (2, 4, 8, 16)
FF = 2816
FT = FF // P
CHUNK = 64
EPS = 1e-6
U0, Q0, K0, V0, QI0, KI0, WI0, QM0, INW = 0, 256, 768, 896, 1024, 1280, 1312, 1320, 1576
GROUPS = ((0, 512), (512, 1024), (1024, 1320), (1320, 1576))
LS = PAST + TS
TOPK_P, TOPK_S = min(256, SEQ // 4), min(256, LS // 4)
SLOT_Q, SLOT_QI, SLOT_QM, SLOT_K, SLOT_KI = 0, 8, 16, 20, 22
NSLOT = 23
MASKED = -1.0e30
UNSEEN, TAKEN, TAKEN_BELOW = -2.0e38, -3.0e38, -2.5e38


class Steps:

    def __init__(self, eng, sem, done=0):
        self.eng, self.sem, self.done = eng, sem, done

    def step(self, instruction):
        instruction.then_inc(self.sem, 1)
        self.done = self.done + 1
        self.eng.wait_ge(self.sem, self.done)


RSQRT_SEED = 1597463007.0


def rsqrt(dve, st, r, v, t, signal=None):
    st.step(dve.tensor_scalar(r.bitcast(I32), v.bitcast(I32), -0.5, RSQRT_SEED, ALU.mult, ALU.add))
    for i in range(4):
        st.step(dve.tensor_tensor(t, r, r, ALU.mult))
        st.step(dve.scalar_tensor_tensor(t, t, -0.5, v, ALU.mult, ALU.mult))
        last = dve.scalar_tensor_tensor(r, t, 1.5, r, ALU.add, ALU.mult)
        if i == 3 and signal is not None:
            last.then_inc(signal, 1)
        else:
            st.step(last)


def flat(ap, pattern):
    return ap.rearrange(pattern)


def squeeze(ap):
    return ap.rearrange("p a n -> p (a n)")


class Pool_:

    def __init__(self, nc, ctx, tag):
        self.nc, self.ctx, self.tag = nc, ctx, tag

    def sb(self, name, shape, dt=F32):
        return self.ctx.enter_context(self.nc.sbuf_tensor(f"{self.tag}_{name}", shape, dt))

    def ps(self, name, shape, dt=F32):
        return self.ctx.enter_context(self.nc.psum_tensor(f"{self.tag}_{name}", shape, dt))

    def sem(self, name):
        return self.ctx.enter_context(self.nc.semaphore(f"{self.tag}_{name}"))


def clear_semaphores(nc):
    with nc.Block() as block:

        @block.gpsimd
        def _(pool):
            used = sorted(nc.released_uncleared_semaphores)
            assert used == list(range(used[0], used[-1] + 1))
            pool.sem_clear(range(used[0], used[-1] + 1))


def phase_memory(nc, t, keep):
    with ExitStack() as ctx:
        m = Pool_(nc, ctx, "mem")
        mem = m.sb("mem", [P, 2, D])
        wraw = m.sb("wraw", [P, KC, 512])
        whi, wlo = m.sb("whi", [P, KC, 512], F32R), m.sb("wlo", [P, KC, 512], F32R)
        gain = m.sb("gain", [P, KC])
        kgain = m.sb("kgain", [P, HD])
        cache_k = m.sb("cache_k", [P, 4, NKV * HD])
        cache_ki = m.sb("cache_ki", [P, 4, ID])
        cache_mk = m.sb("cache_mk", [P, 2, MH * HD])
        junk = m.sb("junk", [P, D])
        ss, rs, tmp = m.sb("ss", [P, 2]), m.sb("rs", [P, 2]), m.sb("tmp", [P, 8])
        ssh, rsh = m.sb("ssh", [P, 8]), m.sb("rsh", [P, 8])
        xhi, xlo = m.sb("xhi", [P, KC, P], F32R), m.sb("xlo", [P, KC, P], F32R)
        kv = m.sb("kv", [P, 2, 512])
        stack = m.sb("stack", [P, 28, P], F32R)
        ps_x, ps_kv, ps_t = m.ps("ps_x", [P, D]), m.ps("ps_kv", [P, 2, 512]), m.ps("ps_t", [P, 2, 512])
        loaded, ident_ready, w_hi, w_lo = m.sem("loaded"), m.sem("ident"), m.sem("w_hi"), m.sem("w_lo")
        squares, xt, x_hi, x_lo, product = m.sem("squares"), m.sem("xt"), m.sem("x_hi"), m.sem("x_lo"), m.sem("product")
        rstd_ready, kv_out, stacked, turned, kept = m.sem("rstd"), m.sem("kv_out"), m.sem("stacked"), m.sem("turned"), m.sem("kept")
        dve_steps, pool_steps, stored = m.sem("dve"), m.sem("pool"), m.sem("stored")
        ident = keep["ident"]
        LOADS = 11
        block = ctx.enter_context(nc.Block())

        @block.sync
        def _(sp):
            loads = [
                (mem[:, :, :], t["mem_prompt"].rearrange("b (m p) d -> p (b m) d", p=P)),
                (wraw[:, :, 0:256], t["w_mem_k"].rearrange("l (c p) n -> p (l c) n", p=P)),
                (wraw[:, :, 256:512], t["w_mem_v"].rearrange("l (c p) n -> p (l c) n", p=P)),
                (gain[:, :], t["mem_norm"].rearrange("l (c p) -> p (l c)", p=P)),
                (kgain[:, :], t["mem_k_norm"].broadcast_to([P, HD])),
                (cache_k[:, :, :], t["cache_k"].rearrange("l b (c p) h d -> p (l b c) (h d)", p=P)),
                (cache_ki[:, :, :], t["cache_kidx"].rearrange("l b (c p) d -> p (l b c) d", p=P)),
                (cache_mk[:, :, :], t["cache_mem_k"].rearrange("l b (c p) h d -> p (l b c) (h d)", p=P)),
                (keep["vs"][:, 0:4, :], t["cache_v"].rearrange("l b (c p) h d -> p (l b c) (h d)", p=P)),
                (keep["mv"][:, 1, :, :], t["cache_mem_v"].rearrange("l b (c p) h d -> p (l b c) (h d)", p=P)),
            ]
            assert len(loads) + 1 == LOADS
            for dst, src in loads:
                sp.dma_start(dst, src, allow_slow_non_contiguous=len(dst.shape) == 2).then_inc(loaded, 16)
            sp.dma_start(keep["pool_scale"][:, :], t["pool_scale"].rearrange("l (c p) -> p (l c)", p=P),
                         allow_slow_non_contiguous=True).then_inc(loaded, 16)
            for i in range(2):
                sp.wait_ge(kv_out, i + 1)
                for n, name in enumerate(("new_mem_k_prompt", "new_mem_v_prompt")):
                    dst = t[name].rearrange("l b (m p) h d -> (l b m) p (h d)", p=P)[i]
                    sp.dma_start(dst, kv[:, i, 256 * n:256 * n + 256]).then_inc(stored, 16)
            sp.wait_ge(stored, 64)

        @block.gpsimd
        def _(pool):
            pool.memset(ident[:, :], 0.0).then_inc(pool_steps, 1)
            pool.wait_ge(pool_steps, 1)
            pool.affine_select(out=ident[:, :], in_=ident[:, :], compare_op=ALU.not_equal, fill=1.0, base=0,
                               pattern=[[-1, P]], channel_multiplier=1).then_inc(ident_ready, 1)

        @block.scalar
        def _(act):
            act.wait_ge(loaded, 16 * LOADS)
            for i in range(2):
                act.activation(junk[:, :], mem[:, i, :], ACT.Square, accum_out=ss[:, i:i + 1]).then_inc(squares, 1)
                act.wait_ge(squares, i + 1)
            for c in range(KC):
                act.activation(whi[:, c, :], wraw[:, c, :], ACT.Identity, scale=gain[:, c:c + 1]).then_inc(w_hi, 1)
            for i in range(2):
                act.wait_ge(xt, i + 1)
                if i:
                    act.wait_ge(product, i)
                for h in range(2):
                    ins = act.activation(xhi[:, 4 * h:4 * h + 4, :], ps_x[:, 512 * h:512 * h + 512].rearrange("p (c n) -> p c n", n=P), ACT.Copy)
                ins.then_inc(x_hi, 1)

        @block.tensor
        def _(pe):
            pe.wait_ge(ident_ready, 1)
            pe.wait_ge(loaded, 16 * LOADS)
            for i in range(2):
                if i:
                    pe.wait_ge(x_lo, i)
                for c in range(KC):
                    ins = pe.transpose(ps_x[:, P * c:P * c + P], mem[:, i, P * c:P * c + P], ident[:, :])
                ins.then_inc(xt, 1)
                pe.wait_ge(x_lo, i + 1)
                pe.wait_ge(w_lo, KC)
                for c in range(KC):
                    for n, (a, b) in enumerate(((xhi, whi), (xhi, wlo), (xlo, whi))):
                        ins = pe.matmul(ps_kv[:, i, :], a[:, c, :], b[:, c, :], start=(c == 0 and n == 0), stop=(c == KC - 1 and n == 2))
                ins.then_inc(product, 1)
            for g in range(7):
                pe.wait_ge(stacked, (1, 2, 3, 4, 5, 5, 6)[g])
                if g >= 2:
                    pe.wait_ge(kept, g - 1)
                for s in range(4):
                    ins = pe.transpose(ps_t[:, g % 2, P * s:P * s + P], stack[:, 4 * g + s, :].bitcast(F32), ident[:, :])
                ins.then_inc(turned, 1)

        @block.vector
        def _(dve):
            st = Steps(dve, dve_steps)
            dve.wait_ge(squares, 2)
            st.step(dve.tensor_scalar(ss[:, :], ss[:, :], 1.0 / D, EPS, ALU.mult, ALU.add))
            rsqrt(dve, st, rs[:, :], ss[:, :], tmp[:, 0:2])
            for c in range(KC):
                dve.wait_ge(w_hi, c + 1)
                dve.scalar_tensor_tensor(wlo[:, c, :], wraw[:, c, :], gain[:, c:c + 1], whi[:, c, :].bitcast(F32),
                                         ALU.mult, ALU.subtract).then_inc(w_lo, 1)
            for i in range(2):
                dve.wait_ge(x_hi, i + 1)
                for h in range(2):
                    ins = dve.tensor_tensor(xlo[:, 4 * h:4 * h + 4, :], ps_x[:, 512 * h:512 * h + 512].rearrange("p (c n) -> p c n", n=P),
                                            xhi[:, 4 * h:4 * h + 4, :].bitcast(F32), ALU.subtract)
                ins.then_inc(x_lo, 1)
            for i in range(2):
                dve.wait_ge(product, i + 1)
                st.step(dve.tensor_scalar(kv[:, i, :], ps_kv[:, i, :], rs[:, i:i + 1], None, ALU.mult))
                keys = kv[:, i, 0:256].rearrange("p (h d) -> p h d", d=HD)
                st.step(dve.tensor_tensor(junk[:, 0:256], kv[:, i, 0:256], kv[:, i, 0:256], ALU.mult))
                st.step(dve.tensor_reduce(ssh[:, 0:4], junk[:, 0:256].rearrange("p (h d) -> p h d", d=HD), AX.X, ALU.add))
                st.step(dve.tensor_scalar(ssh[:, 0:4], ssh[:, 0:4], 1.0 / HD, EPS, ALU.mult, ALU.add))
                rsqrt(dve, st, rsh[:, 0:4], ssh[:, 0:4], tmp[:, 0:4])
                st.step(dve.tensor_tensor(keys, keys, rsh[:, 0:4].unsqueeze(2).broadcast_to([P, 4, HD]), ALU.mult))
                st.step(dve.tensor_tensor(keys, keys, kgain[:, :].unsqueeze(1).broadcast_to([P, 4, HD]), ALU.mult))
                dve.tensor_copy(keep["mv"][:, 0, i, :], kv[:, i, 256:512]).then_inc(kv_out, 1)
                split_rows(dve, st, stack[:, 4 * i:4 * i + 4, :], keys, HD, signal=stacked)
            for i in range(2):
                split_rows(dve, st, stack[:, 8 + 4 * i:12 + 4 * i, :], cache_mk[:, i, :].rearrange("p (h d) -> p h d", d=HD), HD,
                           signal=stacked)
            split_rows(dve, st, stack[:, 16:24, :], cache_k[:, :, :].rearrange("p c (h d) -> p (c h) d", d=HD), HD, signal=stacked)
            split_index(dve, st, stack[:, 24:28, :], cache_ki[:, :, :], key=True, signal=stacked)
            for g in range(7):
                dve.wait_ge(turned, g + 1)
                src = ps_t[:, g % 2, :].rearrange("p (s n) -> p s n", n=P)
                if g < 4:
                    ins = dve.tensor_copy(keep["mkT"][:, g // 2, :, P * (g % 2):P * (g % 2) + P], src)
                elif g < 6:
                    for j in range(NKV):
                        dst = keep["ksT"][:, j, 256 * (g - 4):256 * (g - 4) + 256].rearrange("p (c n) -> p c n", n=P)
                        ins = dve.tensor_copy(dst, ps_t[:, g % 2, :].rearrange("p (c h n) -> p h c n", h=NKV, n=P)[:, j])
                else:
                    ins = dve.tensor_copy(keep["kisT"][:, 0:512], ps_t[:, g % 2, :])
                ins.then_inc(kept, 1)
            dve.wait_ge(kept, 7)


def split_rows(dve, st, out, x, n, signal=None):
    st.step(dve.tensor_copy(out[:, :, 0:n], x))
    last = dve.tensor_tensor(out[:, :, n:2 * n], x, out[:, :, 0:n].bitcast(F32), ALU.subtract)
    if signal is not None:
        last.then_inc(signal, 1)


def split_index(dve, st, out, x, key, signal=None):
    hi, lo = ((0, 2), (1, 3)) if key else ((0, 1), (2, 3))
    part = lambda n: out[:, :, ID * n:ID * n + ID]
    for n in hi:
        first = dve.tensor_copy(part(n), x)
    st.step(first)
    for n in lo:
        last = dve.tensor_tensor(part(n), x, part(hi[0]).bitcast(F32), ALU.subtract)
    if signal is not None:
        last.then_inc(signal, 1)


def phase_project(nc, t, keep):
    with ExitStack() as ctx:
        m = Pool_(nc, ctx, "proj")
        whi, wlo = m.sb("whi", [P, KC, INW], F32R), m.sb("wlo", [P, KC, INW], F32R)
        wraw = m.sb("wraw", [P, 2, INW])
        gain = m.sb("gain", [P, KC])
        hgain = m.sb("hgain", [P, 14, HD])
        x = m.sb("x", [P, 2, D])
        rope = m.sb("rope", [P, 2, 48])
        xhi, xlo = m.sb("xhi", [P, KC, P], F32R), m.sb("xlo", [P, KC, P], F32R)
        pr = m.sb("pr", [P, 2, INW])
        qn = m.sb("qn", [P, 2, 14, HD])
        stack = wraw[:, :, :].rearrange("p a n -> p (a n)")[:, 0:NSLOT * P].rearrange("p (s n) -> p s n", n=P).bitcast(F32R)
        sT = m.sb("sT", [P, NSLOT, P], F32R)
        junk = m.sb("junk", [P, D], mybir.dt.bfloat16)
        rot = m.sb("rot", [P, 2, 10, 16])
        ss, rs, tmp = m.sb("ss", [P, 2]), m.sb("rs", [P, 2]), m.sb("tmp", [P, 16])
        ssh, rsh = m.sb("ssh", [P, 14]), m.sb("rsh", [P, 14])
        u_old, u_old_s = m.sb("u_old", [P, PW]), m.sb("u_old_s", [P, PW])
        band, band0, band_old = m.sb("band", [P, PG, P]), m.sb("band0", [P, PG, P]), m.sb("band_old", [P, PG, P])
        pool_w = m.sb("pool_w", [P, 2, P])
        zT, poolT = m.sb("zT", [P, 2, P]), m.sb("poolT", [P, 2, P])
        ps_x, ps_g, ps_t = m.ps("ps_x", [P, D]), m.ps("ps_g", [P, 4, 512]), m.ps("ps_t", [P, 2, 512])
        consts = m.sem("consts")
        w_loaded, w_hi, w_lo = [m.sem("w_loaded0"), m.sem("w_loaded1")], m.sem("w_hi"), m.sem("w_lo")
        x_loaded = [m.sem("x_loaded0"), m.sem("x_loaded1")]
        rope_loaded = [m.sem("rope_loaded0"), m.sem("rope_loaded1")]
        squares, rstd, xt, x_hi, x_lo = m.sem("squares"), m.sem("rstd"), m.sem("xt"), m.sem("x_hi"), m.sem("x_lo")
        product, product_read, prepared = m.sem("product"), m.sem("product_read"), m.sem("prepared")
        heads_ready, turned, read_act, read_dve = m.sem("heads_ready"), m.sem("turned"), m.sem("read_act"), m.sem("read_dve")
        stored = [m.sem("stored0"), m.sem("stored1")]
        cleared, turned_stored, dve_steps, old_ready, pool_out = m.sem("cleared"), m.sem("turned_stored"), m.sem("dve"), m.sem("old_ready"), m.sem("pool_out")
        ident = keep["ident"]
        NCONST = 12
        STORES = 3
        N_T = 8

        def pipeline(main=None, prepare=None, turn=None, finish=None, loop=None, steps=None):
            stages = [s or (lambda *_: None) for s in (main, prepare, turn, finish)]

            def call(stage, n, u, i):
                stages[stage](n, u, TS if isinstance(n, int) and n == NB else P, i)

            def pair(i):
                for u in range(2):
                    call(0, 2 * i + u + 1, 1 - u, i + u)
                    call(1, 2 * i + u, u, i)
                    call(2, 2 * i + u + 2, u, i + 1)
                    call(3, 2 * i + u, u, i)

            call(2, 0, 0, 0)
            call(0, 0, 0, 0)
            call(2, 1, 1, 0)
            start = steps.done if steps else 0
            pair(0)
            per_pair = steps.done - start if steps else 0
            with loop(1, NB // 2 - 1) as i:
                if steps:
                    steps.done = start + i * per_pair
                pair(i)
            if steps:
                steps.done = start + (NB // 2 - 1) * per_pair
            pair_end = NB // 2 - 1
            n = NB - 2
            call(0, n + 1, 1, pair_end)
            call(1, n, 0, pair_end)
            call(2, n + 2, 0, pair_end + 1)
            call(3, n, 0, pair_end)
            call(0, n + 2, 0, pair_end + 1)
            call(1, n + 1, 1, pair_end)
            call(3, n + 1, 1, pair_end)
            call(1, n + 2, 0, pair_end + 1)
            call(3, n + 2, 0, pair_end + 1)

        def xrows(name_p, name_s, pattern, n, T):
            if T == P:
                return t[name_p].rearrange(pattern, p=P)[bass.ds(n, 1)].rearrange("n p w -> p (n w)")
            return t[name_s].rearrange(pattern, p=TS)[0]

        block = ctx.enter_context(nc.Block())

        @block.sync
        def _(sp):
            sp.wait_ge(cleared, 2)
            for dst, src in (
                (gain[:, :], t["norm1"].rearrange("l (c p) -> p (l c)", p=P)),
                (band[:, :, :], t["band"].rearrange("g p n -> p g n")),
                (band0[:, :, :], t["band_first"].rearrange("g p n -> p g n")),
                (band_old[96:P, :, :], t["band_old"].rearrange("g p n -> p g n")),
                (u_old_s[P - HIST:P, :], t["state_pool"].rearrange("l b r w -> (l b r) w")),
                (hgain[:, 0, :], t["q_norm"].broadcast_to([P, HD])),
                (hgain[:, 8, :], t["k_norm"].broadcast_to([P, HD])),
                (hgain[:, 10, :], t["mem_q_norm"].broadcast_to([P, HD])),
            ):
                sp.dma_start(dst, src, allow_slow_non_contiguous=len(dst.shape) == 2).then_inc(consts, 16)
            for g in range(PG):
                r = HD * (g % 2)
                sp.dma_start(pool_w[r:r + HD, g // 2, r:r + HD], t["pool_w"][0, g]).then_inc(consts, 16)
            for c in range(KC):
                if c >= 2:
                    sp.wait_ge(w_lo, c - 1)
                sp.dma_start(wraw[:, c % 2, :], t["w_in"].rearrange("l (c p) n -> c p (l n)", p=P)[c]).then_inc(w_loaded[c % 2], 16)

            def rows_of(name, n, T, width):
                kind = "prompt" if T == P else "sample"
                flat_rows = t[f"{name}_{kind}"]
                flat_rows = flat_rows.rearrange("l b s d -> (l b s) d") if len(flat_rows.shape) == 4 else flat_rows.rearrange("l b s h d -> (l b s) (h d)")
                return flat_rows[bass.ds(n * P, P)] if T == P else flat_rows

            def store_rows(n, u, T, i):
                sp.wait_ge(heads_ready, n + 1)
                sp.dma_start(rows_of("new_k", n, T, 128), qn[0:T, u, 8:10, :].rearrange("p h d -> p (h d)")).then_inc(stored[u], 16)
                sp.dma_start(rows_of("new_v", n, T, 128), pr[0:T, u, V0:QI0]).then_inc(stored[u], 16)
                sp.dma_start(rows_of("new_kidx", n, T, ID), pr[0:T, u, KI0:WI0]).then_inc(stored[u], 16)

            def store_turned(n, u, T, i):
                sp.wait_ge(read_act, 4 * n + 4)
                sp.wait_ge(read_dve, 4 * n + 4)
                sp.dma_start(t["sT"][bass.ds(n, 1)].rearrange("n p (s w) -> p (n s) w", w=P)[:, :, 0:T], sT[:, :, 0:T].bitcast(F32)).then_inc(turned_stored, 16)
                at = bass.ds(n * P, P) if T == P else slice(SEQ, ROWS)
                sp.dma_start(t["mixT"][0:PW, at].rearrange("(c p) n -> p c n", p=P), poolT[:, :, 0:T]).then_inc(turned_stored, 16)
                if isinstance(n, int) and n >= NB - 1:
                    name = "new_pool_prompt" if T == P else "new_pool_sample"
                    sp.dma_start(t[name].rearrange("l b r w -> (l b r) w"), pr[T - HIST:T, u, U0:Q0]).then_inc(pool_out, 16)

            pipeline(prepare=store_rows, finish=store_turned, loop=sp.Fori)
            sp.wait_ge(stored[0], 16 * STORES * (NB // 2 + 1))
            sp.wait_ge(stored[1], 16 * STORES * (NB // 2))
            sp.wait_ge(turned_stored, 32 * (NB + 1))
            sp.wait_ge(pool_out, 32)

        @block.gpsimd
        def _(pool):
            pool.memset(pool_w[:, :, :], 0.0).then_inc(cleared, 1)
            pool.memset(u_old_s[:, :], 0.0).then_inc(cleared, 1)

            def load(n, u, T, i, first=False):
                if not first:
                    pool.wait_ge(xt, n - 1)
                    pool.wait_ge(squares, n - 1)
                pool.dma_start(x[0:T, u, :], xrows("x_prompt", "x_sample", "b (n p) d -> (b n) p d", n, T)).then_inc(x_loaded[u], 16)
                if not first:
                    pool.wait_ge(prepared, n - 1)
                if T == P:
                    src = t["rope_table"][0:SEQ].rearrange("(n p) w -> n p w", p=P)[bass.ds(n, 1)].rearrange("n p w -> p (n w)")
                else:
                    src = t["rope_table"][PAST:LS]
                pool.dma_start(rope[0:T, u, :], src).then_inc(rope_loaded[u], 16)

            load(0, 0, P, 0, first=True)
            load(1, 1, P, 0, first=True)
            with pool.Fori(1, NB // 2) as i:
                for u in range(2):
                    load(2 * i + u, u, P, i)
            load(NB, 0, TS, 0)

        @block.scalar
        def _(act):
            act.wait_ge(consts, 16 * NCONST)
            for c in range(KC):
                act.wait_ge(w_loaded[c % 2], 16 * (c // 2 + 1))
                act.activation(whi[:, c, :], wraw[:, c % 2, :], ACT.Identity, scale=gain[:, c:c + 1]).then_inc(w_hi, 1)

            def turn(n, u, T, i):
                act.wait_ge(x_loaded[u], 16 * (i + 1))
                act.wait_ge(squares, n)
                act.activation(junk[0:T, :], x[0:T, u, :], ACT.Square, accum_out=ss[0:T, u:u + 1]).then_inc(squares, 1)
                act.wait_ge(xt, n + 1)
                for h in range(2):
                    ins = act.activation(xhi[:, 4 * h:4 * h + 4, 0:T], ps_x[:, 512 * h:512 * h + 512].rearrange("p (c n) -> p c n", n=P)[:, :, 0:T], ACT.Copy)
                ins.then_inc(x_hi, 1)

            def scale(n, u, T, i):
                act.wait_ge(rstd, n + 1)
                if not (isinstance(n, int) and n < 2):
                    act.wait_ge(stored[u], 16 * STORES * i)
                    act.wait_ge(turned, N_T * (n - 1))
                    act.wait_ge(old_ready, n)
                for g, (a, b) in enumerate(GROUPS):
                    act.wait_ge(product, 4 * n + g + 1)
                    act.activation(pr[0:T, u, a:b], ps_g[0:T, g, 0:b - a], ACT.Identity, scale=rs[0:T, u:u + 1]).then_inc(product_read, 1)

            def place(n, u, T, i):
                act.wait_ge(turned_stored, 32 * n)
                for g in (0, 2, 4):
                    act.wait_ge(turned, N_T * n + g + 1)
                    src = ps_t[:, 0, :].rearrange("p (s n) -> p s n", n=P)[:, :, 0:T]
                    act.activation(sT[:, 4 * g:4 * g + 4, 0:T], src, ACT.Copy).then_inc(read_act, 1)
                act.wait_ge(turned, N_T * n + 7)
                act.activation(zT[:, :, 0:T], ps_t[:, 0, 0:256].rearrange("p (s n) -> p s n", n=P)[:, :, 0:T], ACT.Copy).then_inc(read_act, 1)

            pipeline(main=scale, turn=turn, finish=place, loop=act.Fori)

        @block.tensor
        def _(pe):
            pe.wait_ge(consts, 16 * NCONST)

            def turn(n, u, T, i):
                pe.wait_ge(x_loaded[u], 16 * (i + 1))
                pe.wait_ge(x_lo, n)
                for c in range(KC):
                    ins = pe.transpose(ps_x[:, P * c:P * c + T], x[0:T, u, P * c:P * c + P], ident[0:T, 0:T])
                ins.then_inc(xt, 1)

            def product_of(n, u, T, i):
                pe.wait_ge(x_lo, n + 1)
                if isinstance(n, int) and n == 0:
                    pe.wait_ge(w_lo, KC)
                for g, (a, b) in enumerate(GROUPS):
                    if not (isinstance(n, int) and n == 0):
                        pe.wait_ge(product_read, 4 * (n - 1) + g + 1)
                    for c in range(KC):
                        for k, (p, q) in enumerate(((xhi, whi), (xhi, wlo), (xlo, whi))):
                            ins = pe.matmul(ps_g[0:T, g, 0:b - a], p[:, c, 0:T], q[:, c, a:b], start=(c == 0 and k == 0), stop=(c == KC - 1 and k == 2))
                    ins.then_inc(product, 1)

            def turn_stack(n, u, T, i):
                pe.wait_ge(prepared, n + 1)
                for g in range(6):
                    if g >= 2:
                        pe.wait_ge((read_act, read_dve)[g % 2], 4 * n + g // 2)
                    else:
                        pe.wait_ge((read_act, read_dve)[g % 2], 4 * n)
                    for s in range(min(4, NSLOT - 4 * g)):
                        ins = pe.transpose(ps_t[:, g % 2, P * s:P * s + T], stack[0:T, 4 * g + s, :].bitcast(F32), ident[0:T, 0:T])
                    ins.then_inc(turned, 1)
                pe.wait_ge(read_act, 4 * n + 3)
                pe.wait_ge(old_ready, n + 1)
                first = isinstance(n, int) and n == 0
                old = u_old_s if T == TS else u_old
                for g in range(PG):
                    out = ps_t[HD * (g % 2):HD * (g % 2) + HD, 0, P * (g // 2):P * (g // 2) + T]
                    pe.matmul(out, pr[0:T, u, HD * g:HD * g + HD], (band0 if first else band)[0:T, g, 0:T], start=True, stop=False)
                    ins = pe.matmul(out, old[96:P, HD * g:HD * g + HD], band_old[96:P, g, 0:T], start=False, stop=True)
                ins.then_inc(turned, 1)
                pe.wait_ge(read_act, 4 * n + 4)
                pe.wait_ge(read_dve, 4 * n + 3)
                for c in range(2):
                    ins = pe.matmul(ps_t[:, 1, P * c:P * c + T], pool_w[:, c, :], zT[:, c, 0:T], start=True, stop=True)
                ins.then_inc(turned, 1)

            pipeline(main=product_of, turn=turn, finish=turn_stack, loop=pe.Fori)

        @block.vector
        def _(dve):
            st = Steps(dve, dve_steps)
            dve.wait_ge(consts, 16 * NCONST)
            st.step(dve.memset(u_old[:, :], 0.0))
            dve.memset(tmp[:, :], 0.0).then_inc(old_ready, 1)
            st.step(dve.tensor_scalar(hgain[:, 0, :], hgain[:, 0, :], HD ** -0.5, None, ALU.mult))
            st.step(dve.tensor_scalar(hgain[:, 10, :], hgain[:, 10, :], HD ** -0.5, None, ALU.mult))
            for a, b in ((0, 8), (8, 10), (10, 14)):
                st.step(dve.tensor_copy(hgain[:, a + 1:b, :], hgain[:, a:a + 1, :].broadcast_to([P, b - a - 1, HD])))
            for c in range(KC):
                dve.wait_ge(w_hi, c + 1)
                dve.scalar_tensor_tensor(wlo[:, c, :], wraw[:, c % 2, :], gain[:, c:c + 1], whi[:, c, :].bitcast(F32),
                                         ALU.mult, ALU.subtract).then_inc(w_lo, 1)

            def turn(n, u, T, i):
                dve.wait_ge(squares, n + 1)
                st.step(dve.tensor_scalar(ss[0:T, u:u + 1], ss[0:T, u:u + 1], 1.0 / D, EPS, ALU.mult, ALU.add))
                rsqrt(dve, st, rs[0:T, u:u + 1], ss[0:T, u:u + 1], tmp[0:T, 0:1], signal=rstd)
                dve.wait_ge(x_hi, n + 1)
                for h in range(2):
                    ins = dve.tensor_tensor(xlo[:, 4 * h:4 * h + 4, 0:T], ps_x[:, 512 * h:512 * h + 512].rearrange("p (c n) -> p c n", n=P)[:, :, 0:T],
                                            xhi[:, 4 * h:4 * h + 4, 0:T].bitcast(F32), ALU.subtract)
                ins.then_inc(x_lo, 1)

            def rotate(x1, x2, both, cos, sin, w):
                T, heads, half = x1.shape
                a, b = rot[0:T, 0, 0:heads, 0:2 * half], rot[0:T, 1, 0:heads, 0:2 * half]
                dve.tensor_tensor(a, both, cos.unsqueeze(1).broadcast_to([T, heads, 2 * half]), ALU.mult)
                dve.tensor_tensor(b[:, :, 0:half], x2, sin[:, 0:half].unsqueeze(1).broadcast_to([T, heads, half]), ALU.mult)
                st.step(dve.tensor_tensor(b[:, :, half:], x1, sin[:, half:].unsqueeze(1).broadcast_to([T, heads, half]), ALU.mult))
                last = dve.tensor_tensor(both, a, b, ALU.add)
                st.step(last)

            def prepare(n, u, T, i):
                row = pr[0:T, u, :]
                heads = qn[0:T, u, :, :]
                dve.wait_ge(product_read, 4 * n + 4)
                if not (isinstance(n, int) and n < 2):
                    dve.wait_ge(stored[u], 16 * STORES * i)
                ki_row = row[:, KI0:WI0]
                square = heads.rearrange("p h d -> p (h d)")
                dve.tensor_tensor(square[:, 0:640], row[:, Q0:V0], row[:, Q0:V0], ALU.mult)
                st.step(dve.tensor_tensor(square[:, 640:896], row[:, QM0:INW], row[:, QM0:INW], ALU.mult))
                st.step(dve.tensor_reduce(ssh[0:T, :], heads, AX.X, ALU.add))
                st.step(dve.tensor_scalar(ssh[0:T, :], ssh[0:T, :], 1.0 / HD, EPS, ALU.mult, ALU.add))
                rsqrt(dve, st, rsh[0:T, :], ssh[0:T, :], tmp[0:T, 0:14])
                dve.tensor_tensor(heads[:, 0:10, :], row[:, Q0:V0].rearrange("p (h d) -> p h d", d=HD),
                                  rsh[0:T, 0:10].unsqueeze(2).broadcast_to([T, 10, HD]), ALU.mult)
                st.step(dve.tensor_tensor(heads[:, 10:14, :], row[:, QM0:INW].rearrange("p (h d) -> p h d", d=HD),
                                          rsh[0:T, 10:14].unsqueeze(2).broadcast_to([T, 4, HD]), ALU.mult))
                st.step(dve.tensor_tensor(heads, heads, hgain[0:T, :, :], ALU.mult))
                dve.wait_ge(rope_loaded[u], 16 * (i + 1))
                rotate(heads[:, 0:10, 0:8], heads[:, 0:10, 8:16], heads[:, 0:10, 0:16], rope[0:T, u, 0:16], rope[0:T, u, 16:32], 16)
                qi = row[:, QI0:WI0].rearrange("p (h d) -> p h d", d=ID)
                rotate(qi[:, :, 0:4], qi[:, :, 4:8], qi[:, :, 0:8], rope[0:T, u, 32:40], rope[0:T, u, 40:48], 8)
                w_at = keep["w8"][0:T, bass.ds(n, 1), :].rearrange("p n h -> p (n h)")
                dve.tensor_scalar(w_at, row[:, WI0:QM0], (IH * ID) ** -0.5, None, ALU.mult).then_inc(heads_ready, 1)
                split_rows(dve, st, stack[0:T, SLOT_Q:SLOT_Q + 8, :], heads[:, 0:8, :], HD)
                split_rows(dve, st, stack[0:T, SLOT_K:SLOT_K + 2, :], heads[:, 8:10, :], HD)
                split_rows(dve, st, stack[0:T, SLOT_QM:SLOT_QM + 4, :], heads[:, 10:14, :], HD)
                split_index(dve, st, stack[0:T, SLOT_QI:SLOT_QI + 8, :], qi[:, 0:8, :], key=False)
                split_index(dve, st, stack[0:T, SLOT_KI:SLOT_KI + 1, :], qi[:, 8:9, :], key=True, signal=prepared)

            def place(n, u, T, i):
                dve.wait_ge(turned_stored, 32 * n)
                src = ps_t[:, 1, :].rearrange("p (s n) -> p s n", n=P)[:, :, 0:T]
                for g in (1, 3, 5):
                    k = min(4, NSLOT - 4 * g)
                    dve.wait_ge(turned, N_T * n + g + 1)
                    dve.tensor_copy(sT[:, 4 * g:4 * g + k, 0:T], src[:, 0:k, :]).then_inc(read_dve, 1)
                dve.wait_ge(turned, N_T * n + 8)
                for c in range(2):
                    ins = dve.tensor_scalar(poolT[:, c, 0:T], src[:, c, :], keep["pool_scale"][:, c:c + 1], None, ALU.mult)
                ins.then_inc(read_dve, 1)
                if T == P:
                    dve.tensor_copy(u_old[96:P, :], pr[96:P, u, U0:Q0]).then_inc(old_ready, 1)

            pipeline(prepare=prepare, turn=turn, finish=place, loop=dve.Fori, steps=st)



def segments(width):
    count = -(-width // 512)
    size = -(-width // count)
    size += size % 2
    return [(a, min(a + size, width)) for a in range(0, width, size)]


class Rows:

    def __init__(self, n):
        self.n, self.sample = n, n == NB
        self.T = TS if self.sample else P
        self.S = LS if self.sample else P * (n + 1)
        self.segs = segments(self.S)
        self.tiles = [(a, min(a + P, self.S)) for a in range(0, self.S, P)]
        self.keep = TOPK_S if self.sample else (TOPK_P if self.S > TOPK_P else 0)
        self.groups = [self.tiles[a:a + 4] for a in range(0, len(self.tiles), 4)]
        self.at = SEQ if self.sample else P * n


BLOCKS = [Rows(n) for n in range(NB + 1)]


def phase_attend(nc, t, keep):
    with ExitStack() as ctx:
        m = Pool_(nc, ctx, "att")
        kT, kiT = m.sb("kT", [P, NKV, SEQ], F32R), m.sb("kiT", [P, SEQ], F32R)
        v = m.sb("v", [P, NB, NKV * HD])
        qa = m.sb("qa", [P, 2, SLOT_K, P], F32R)
        qb = m.sb("qb", [P, 2, 12, P], F32R)
        diag = m.sb("diag", [P, IH, P])
        relu = m.sb("relu", [P, 3, 512])
        scores, work = m.sb("scores", [P, SEQ]), m.sb("work", [P, SEQ])
        mask = m.sb("mask", [P, 2, SEQ])
        probs = m.sb("probs", [P, 2, SEQ])
        pT = m.sb("pT", [P, 2, NB, P])
        top, idle = m.sb("top", [P, 8]), m.sb("idle", [P, 1])
        peaks, neg = m.sb("peaks", [P, 2, 4]), m.sb("neg", [P, 2, 12])
        sums, inv = m.sb("sums", [P, 2, 12]), m.sb("inv", [P, 2, 12])
        rows = m.sb("rows", [P, 768])
        rowsT = m.sb("rowsT", [P, 6, P])
        ps_i, ps_s, ps_l = m.ps("ps_i", [P, 2, 512]), m.ps("ps_s", [P, 512]), m.ps("ps_l", [P, 2, 512])
        ps_p, ps_o = m.ps("ps_p", [P, 2, 512]), m.ps("ps_o", [P, 512])
        keys_loaded, q_loaded = m.sem("keys_loaded"), [m.sem("q_loaded0"), m.sem("q_loaded1")]
        diag_ready, raw_scores, relu_ready = m.sem("diag_ready"), m.sem("raw_scores"), m.sem("relu_ready")
        seg_summed, seg_kept, scores_taken = m.sem("seg_summed"), m.sem("seg_kept"), m.sem("scores_taken")
        logits, masked, neg_ready, exp_done = m.sem("logits"), m.sem("masked"), m.sem("neg_ready"), m.sem("exp_done")
        turned, copied, pv_done, rows_ready = m.sem("turned"), [m.sem("copied_act"), m.sem("copied_dve")], m.sem("pv_done"), m.sem("rows_ready")
        stored, dve_steps = m.sem("stored"), m.sem("dve")
        ident = keep["ident"]
        KEY_LOADS, Q_LOADS = 7, 5
        NHEADS = NH + 1

        segs_before, groups_before = [0], [0]
        for b in BLOCKS:
            segs_before.append(segs_before[-1] + len(b.segs))
            groups_before.append(groups_before[-1] + NH * len(b.groups) + 4)

        def group_index(b, h, g):
            return groups_before[b.n] + (h * len(b.groups) + g if h <= NH else NH * len(b.groups) + 2 + g)

        def bank_reads(index):
            return index % 2, index // 2 + 1

        def logit_count(b, h, s):
            return NH * segs_before[b.n] + b.n + h * len(b.segs) + s

        def copy_groups(eng, e, b, h):
            count = len(b.groups) if h < NH else 2
            for g in range(count):
                index = group_index(b, h, g)
                if index % 2 != e:
                    continue
                eng.wait_ge(turned, index + 1)
                if h == 9:
                    tiles, dst = (4, 2)[g], rowsT[:, 4 * g:4 * g + (4, 2)[g], 0:b.T]
                    if b.n:
                        eng.wait_ge(stored, 16 * b.n)
                    pieces = [(P, dst, ps_p[:, e, 0:P * tiles])]
                else:
                    seq = NHEADS * b.n + h
                    if seq >= 2:
                        eng.wait_ge(pv_done, seq - 1 if h else seq)
                    tiles = b.groups[g] if h < NH else [(0, P)] * 4
                    full = sum(hi - lo == P for lo, hi in tiles)
                    pieces = [(P, pT[:, h % 2, 4 * g:4 * g + full, 0:b.T], ps_p[:, e, 0:P * full])] if full else []
                    if full < len(tiles):
                        w = tiles[-1][1] - tiles[-1][0]
                        pieces.append((w, pT[0:w, h % 2, 4 * g + full:4 * g + full + 1, 0:b.T], ps_p[0:w, e, P * full:P * full + P]))
                for w, dst, src in pieces:
                    src = src.rearrange("p (s n) -> p s n", n=P)[:, :, 0:b.T]
                    ins = eng.activation(dst, src, ACT.Copy) if e == 0 else eng.tensor_copy(dst, src)
                ins.then_inc(copied[e], 1)

        block = ctx.enter_context(nc.Block())

        @block.sync
        def _(sp):
            sT = t["sT"].rearrange("n p (s w) -> s p n w", w=P)
            for j in range(NKV):
                sp.dma_start(kT[:, j, :].rearrange("p (n w) -> p n w", w=P).bitcast(F32), sT[SLOT_K + j, :, 0:NB]).then_inc(keys_loaded, 16)
            sp.dma_start(kiT[:, :].rearrange("p (n w) -> p n w", w=P).bitcast(F32), sT[SLOT_KI, :, 0:NB]).then_inc(keys_loaded, 16)
            last = t["sT"][NB].rearrange("p (s w) -> p s w", w=P)
            sp.dma_start(keep["ksT"][:, :, PAST:LS].bitcast(F32), last[:, SLOT_K:SLOT_KI, 0:TS]).then_inc(keys_loaded, 16)
            sp.dma_start(keep["kisT"][:, PAST:LS].bitcast(F32), last[:, SLOT_KI, 0:TS]).then_inc(keys_loaded, 16)
            sp.dma_start(v[:, :, :], t["new_v_prompt"].rearrange("l b (n p) h d -> p (l b n) (h d)", p=P)).then_inc(keys_loaded, 16)
            sp.dma_start(keep["vs"][0:TS, 4, :], t["new_v_sample"].rearrange("l b s h d -> (l b s) (h d)")).then_inc(keys_loaded, 16)

            def load(b):
                u = b.n % 2
                if b.n >= 2:
                    sp.wait_ge(pv_done, NHEADS * (b.n - 1))
                src = t["sT"][b.n].rearrange("p (s w) -> p s w", w=P)
                sp.dma_start(qa[:, u, :, 0:b.T].bitcast(F32), src[:, 0:SLOT_K, 0:b.T]).then_inc(q_loaded[u], 16)
                for lo, hi in ((0, HD), (HD, P)):
                    for a, slot, count in ((0, SLOT_Q, 8), (8, SLOT_QM, 4)):
                        sp.dma_start(qb[lo:hi, u, a:a + count, 0:b.T].bitcast(F32), src[P - hi:P - lo, slot:slot + count, 0:b.T]).then_inc(q_loaded[u], 16)

            load(BLOCKS[0])
            load(BLOCKS[1])
            for b in BLOCKS:
                for g in range(2):
                    e, count = bank_reads(group_index(b, 9, g))
                    sp.wait_ge(copied[e], count)
                sp.dma_start(t["mixT"][PW:D, b.at:b.at + b.T].rearrange("(c p) n -> p c n", p=P), rowsT[:, :, 0:b.T]).then_inc(stored, 16)
                if b.n + 2 <= NB:
                    load(BLOCKS[b.n + 2])
            sp.wait_ge(stored, 16 * len(BLOCKS))

        @block.gpsimd
        def _(pool):
            for b in BLOCKS:
                if b.n:
                    pool.wait_ge(seg_summed, segs_before[b.n])
                for h in range(IH):
                    ins = pool.tensor_scalar(diag[0:b.T, h, 0:b.T], ident[0:b.T, 0:b.T], keep["w8"][0:b.T, b.n, h:h + 1], None, ALU.mult)
                ins.then_inc(diag_ready, 1)

        @block.tensor
        def _(pe):
            def index_scores(b):
                u, T = b.n % 2, b.T
                keys = keep["kisT"] if b.sample else kiT
                pe.wait_ge(q_loaded[u], 16 * Q_LOADS * (b.n // 2 + 1))
                pe.wait_ge(diag_ready, b.n + 1)
                pieces = [(s, h) for s in range(len(b.segs)) for h in range(IH)]
                first = IH * segs_before[b.n]

                def raw(i):
                    s, h = pieces[i]
                    lo, hi = b.segs[s]
                    if first + i >= 2:
                        pe.wait_ge(relu_ready, first + i - 1)
                    pe.matmul(ps_i[0:T, (first + i) % 2, 0:hi - lo], qa[:, u, SLOT_QI + h, 0:T], keys[:, lo:hi],
                              start=True, stop=True).then_inc(raw_scores, 1)

                raw(0)
                for i, (s, h) in enumerate(pieces):
                    if i + 1 < len(pieces):
                        raw(i + 1)
                    lo, hi = b.segs[s]
                    if h == 0:
                        pe.wait_ge(seg_kept, segs_before[b.n] + s)
                    pe.wait_ge(relu_ready, first + i + 1)
                    ins = pe.matmul(ps_s[0:T, 0:hi - lo], diag[0:T, h, 0:T], relu[0:T, (first + i) % 3, 0:hi - lo], start=(h == 0), stop=(h == IH - 1))
                    if h == IH - 1:
                        ins.then_inc(seg_summed, 1)

            def head_logits(b, h):
                u, T = b.n % 2, b.T
                if h == NH:
                    pe.wait_ge(masked, logit_count(b, NH, 0))
                    for mh in range(MH):
                        out = ps_l[0:T, mh // 2, 256 * (mh % 2):256 * (mh % 2) + 256]
                        keys = keep["mkT"][:, 1 if b.sample else 0, mh, :]
                        pe.matmul(out, qa[:, u, SLOT_QM + mh, 0:T], keys, start=True, stop=False)
                        ins = pe.matmul(out, qb[:, u, 8 + mh, 0:T], keys, start=False, stop=True)
                    ins.then_inc(logits, 1)
                    return
                keys = keep["ksT"] if b.sample else kT
                for s, (lo, hi) in enumerate(b.segs):
                    n = logit_count(b, h, s)
                    if n >= 2:
                        pe.wait_ge(masked, n - 1)
                    if h == 0 and s < 2 and b.n:
                        pe.wait_ge(exp_done, NHEADS * b.n)
                    out = ps_l[0:T, n % 2, 0:hi - lo]
                    pe.matmul(out, qa[:, u, SLOT_Q + h, 0:T], keys[:, h // GQ, lo:hi], start=True, stop=False)
                    pe.matmul(out, qb[:, u, h, 0:T], keys[:, h // GQ, lo:hi], start=False, stop=True).then_inc(logits, 1)

            def turn_group(index, pieces, T):
                e, count = bank_reads(index)
                if count > 1:
                    pe.wait_ge(copied[e], count - 1)
                for i, (src, width) in enumerate(pieces):
                    ins = pe.transpose(ps_p[0:width, e, P * i:P * i + T], src, ident[0:T, 0:T])
                ins.then_inc(turned, 1)

            def head_values(b, h):
                u, T = b.n % 2, b.T
                seq = NHEADS * b.n + h
                pe.wait_ge(exp_done, seq + 1)
                if h < NH:
                    groups, src = b.groups, probs[0:T, h % 2, :]
                else:
                    groups = [[(P * i, P * i + P) for i in range(4 * g, 4 * g + 4)] for g in range(2)]
                    src = probs[0:T, h % 2, :]

                def turn(g):
                    turn_group(group_index(b, h, g), [(src[:, lo:hi], hi - lo) for lo, hi in groups[g]], T)

                def multiply(g):
                    e, count = bank_reads(group_index(b, h, g))
                    pe.wait_ge(copied[e], count)
                    if g == 0 and h % GQ == 0:
                        pe.wait_ge(rows_ready, 3 * b.n + h // GQ)
                    for i, (lo, hi) in enumerate(groups[g]):
                        k = 4 * g + i
                        if h < NH:
                            values = (keep["vs"] if b.sample else v)[0:hi - lo, k, :]
                            slot, first, last = h % GQ, k == 0, k == len(b.tiles) - 1
                        else:
                            slot, tile = k // 2, k % 2
                            values = keep["mv"][:, 1 if b.sample else 0, tile, P * (slot // 2):P * (slot // 2) + P]
                            first, last = tile == 0, tile == 1
                        ins = pe.matmul(ps_o[0:T, P * slot:P * slot + P], pT[0:hi - lo, h % 2, k, 0:T], values, start=first, stop=last)
                    return ins

                turn(0)
                for g in range(len(groups)):
                    if g + 1 < len(groups):
                        turn(g + 1)
                    ins = multiply(g)
                ins.then_inc(pv_done, 1)

            pe.wait_ge(keys_loaded, 16 * KEY_LOADS)
            index_scores(BLOCKS[0])
            for b in BLOCKS:
                if not b.sample:
                    index_scores(BLOCKS[b.n + 1])
                head_logits(b, 0)
                for h in range(NHEADS):
                    if h + 1 < NHEADS:
                        head_logits(b, h + 1)
                    head_values(b, h)
                pe.wait_ge(rows_ready, 3 * b.n + 3)
                for g, pieces in enumerate(((0, 1, 2, 3), (4, 5))):
                    turn_group(group_index(b, 9, g), [(rows[0:b.T, P * c:P * c + P], P) for c in pieces], b.T)

        @block.scalar
        def _(act):
            def index_relu(b):
                first, T = IH * segs_before[b.n], b.T
                for s, (lo, hi) in enumerate(b.segs):
                    for h in range(IH):
                        i = first + IH * s + h
                        act.wait_ge(raw_scores, i + 1)
                        act.activation(relu[0:T, i % 3, 0:hi - lo], ps_i[0:T, i % 2, 0:hi - lo], ACT.Relu).then_inc(relu_ready, 1)
                    act.wait_ge(seg_summed, segs_before[b.n] + s + 1)
                    if s == 0 and b.n:
                        act.wait_ge(scores_taken, b.n)
                    act.activation(scores[0:T, lo:hi], ps_s[0:T, 0:hi - lo], ACT.Copy).then_inc(seg_kept, 1)

            def exponentials(b, h):
                u, T = b.n % 2, b.T
                act.wait_ge(neg_ready, NHEADS * b.n + h + 1)
                if h < NH:
                    row = probs[0:T, h % 2, 0:b.S]
                    act.activation(row, row, ACT.Exp, bias=neg[0:T, u, h:h + 1], accum_out=sums[0:T, u, h:h + 1]).then_inc(exp_done, 1)
                    return
                last = group_index(b, NH - 2, len(b.groups) - 1)
                act.wait_ge(turned, last + 1)
                for mh in range(MH):
                    ins = act.activation(probs[0:T, h % 2, 256 * mh:256 * mh + 256], ps_l[0:T, mh // 2, 256 * (mh % 2):256 * (mh % 2) + 256],
                                         ACT.Exp, bias=neg[0:T, u, 8 + mh:9 + mh], accum_out=sums[0:T, u, 8 + mh:9 + mh])
                ins.then_inc(exp_done, 1)

            index_relu(BLOCKS[0])
            for b in BLOCKS:
                if not b.sample:
                    index_relu(BLOCKS[b.n + 1])
                exponentials(b, 0)
                for h in range(NHEADS):
                    if h + 1 < NHEADS:
                        exponentials(b, h + 1)
                    copy_groups(act, 0, b, h)
                copy_groups(act, 0, b, 9)

        @block.vector
        def _(dve):
            st = Steps(dve, dve_steps)

            def pick(b, part):
                T, S = b.T, b.S
                cur, at = work[0:T, 0:S], mask[0:T, b.n % 2, 0:S]
                if part == 0:
                    dve.wait_ge(seg_kept, segs_before[b.n + 1])
                    if not b.keep:
                        st.step(dve.memset(at, 0.0))
                        dve.memset(mask[0:CHUNK, b.n % 2, S - CHUNK:S], MASKED).then_inc(scores_taken, 1)
                        dve.wait_ge(scores_taken, b.n + 1)
                        return
                    if not b.sample:
                        st.step(dve.memset(scores[0:CHUNK, S - CHUNK:S], UNSEEN))
                    st.step(dve.max(top[0:T, :], scores[0:T, 0:S]))
                    dve.match_replace(cur, top[0:T, :], scores[0:T, 0:S], TAKEN).then_inc(scores_taken, 1)
                    dve.wait_ge(scores_taken, b.n + 1)
                if not b.keep:
                    return
                total = b.keep // 8 - 1
                rounds = total * (part + 1) // 8 - total * part // 8
                if rounds:
                    start = st.done
                    with dve.Fori(0, rounds) as i:
                        st.done = start + 2 * i
                        st.step(dve.max(top[0:T, :], cur))
                        dve.memset(idle[:, :], 0.0)
                        st.step(dve.match_replace(cur, top[0:T, :], cur, TAKEN))
                    st.done = start + 2 * rounds
                if part == 7:
                    st.step(dve.tensor_scalar(at, cur, TAKEN_BELOW, MASKED, ALU.is_ge, ALU.mult))

            def mask_logits(b, h):
                u, T = b.n % 2, b.T
                first = logit_count(b, h, 0)
                if h == NH:
                    dve.wait_ge(logits, first + 1)
                    for half in range(2):
                        ins = dve.tensor_reduce(neg[0:T, u, 8 + 2 * half:10 + 2 * half], ps_l[0:T, half, :].rearrange("p (h n) -> p h n", n=MT), AX.X, ALU.max)
                    ins.then_inc(masked, 1)
                    dve.wait_ge(masked, first + 1)
                    dve.tensor_scalar(neg[0:T, u, 8:12], neg[0:T, u, 8:12], -1.0, None, ALU.mult).then_inc(neg_ready, 1)
                    return
                if h >= 2 or b.n:
                    if h >= 2:
                        last = group_index(b, h - 2, len(b.groups) - 1)
                    elif h == 0:
                        last = group_index(BLOCKS[b.n - 1], 8, 1)
                    else:
                        last = group_index(BLOCKS[b.n - 1], 7, len(BLOCKS[b.n - 1].groups) - 1)
                    dve.wait_ge(turned, last + 1)
                for s, (lo, hi) in enumerate(b.segs):
                    dve.wait_ge(logits, first + s + 1)
                    dve.tensor_tensor_reduce(probs[0:T, h % 2, lo:hi], ps_l[0:T, (first + s) % 2, 0:hi - lo], mask[0:T, u, lo:hi],
                                             1.0, -3.0e38, ALU.add, ALU.max, peaks[0:T, h % 2, s:s + 1]).then_inc(masked, 1)
                dve.wait_ge(masked, first + len(b.segs))
                st.step(dve.tensor_reduce(neg[0:T, u, h:h + 1], peaks[0:T, h % 2, 0:len(b.segs)], AX.X, ALU.max))
                dve.tensor_scalar(neg[0:T, u, h:h + 1], neg[0:T, u, h:h + 1], -1.0, None, ALU.mult).then_inc(neg_ready, 1)

            def divide(b, q):
                u, T = b.n % 2, b.T
                dve.wait_ge(pv_done, NHEADS * b.n + (GQ * (q + 1) if q < 2 else NHEADS))
                if q == 0 and b.n:
                    dve.wait_ge(turned, groups_before[b.n])
                st.step(dve.reciprocal(inv[0:T, u, 4 * q:4 * q + 4], sums[0:T, u, 4 * q:4 * q + 4]))
                src = ps_o[0:T, :].rearrange("p (h d) -> p h d", d=P)
                dst = rows[0:T, 256 * q:256 * q + 256].rearrange("p (h d) -> p h d", d=HD)
                scale = inv[0:T, u, 4 * q:4 * q + 4].unsqueeze(2).broadcast_to([T, 4, HD])
                if q < 2:
                    dve.tensor_tensor(dst, src[:, :, HD * q:HD * q + HD], scale, ALU.mult).then_inc(rows_ready, 1)
                    return
                for mh in range(MH):
                    o = HD * (mh % 2)
                    ins = dve.tensor_tensor(dst[:, mh], src[:, mh, o:o + HD], scale[:, mh], ALU.mult)
                ins.then_inc(rows_ready, 1)

            for part in range(8):
                pick(BLOCKS[0], part)
            for b in BLOCKS:
                mask_logits(b, 0)
                for h in range(NHEADS):
                    if h + 1 < NHEADS:
                        mask_logits(b, h + 1)
                    if h < 8 and not b.sample:
                        pick(BLOCKS[b.n + 1], h)
                    copy_groups(dve, 1, b, h)
                    if h in (3, 7, 8):
                        divide(b, h // GQ)
                copy_groups(dve, 1, b, 9)



HALF = ROWS // 2
NS, SUB = 3, HALF // 3
PROMPT_1 = SEQ - HALF
EDGES = [(a, min(a + P, HALF)) for a in range(0, HALF, P)]


def first(i):
    return isinstance(i, int) and i == 0


def iterations(eng, body, count, steps=None):
    start = steps.done if steps else 0
    body(0)
    per = steps.done - start if steps else 0
    with eng.Fori(1, count) as i:
        if steps:
            steps.done = start + i * per
        body(i)
    if steps:
        steps.done = start + count * per


def row_tiles(ch, starts):
    tiles = []
    cuts = sorted(set(starts) | ({PROMPT_1} if ch else set()) | {HALF})
    for lo, hi in zip(cuts[:-1], cuts[1:]):
        for a in range(lo, hi, P):
            w = min(P, hi - a)
            sample = ch == 1 and a >= PROMPT_1
            tiles.append((a, w, "sample" if sample else "prompt", a - PROMPT_1 if sample else HALF * ch + a))
    return tiles


def phase_mix(nc, t, ch, ident, ones, hT, nhi, nlo):
    with ExitStack() as ctx:
        m = Pool_(nc, ctx, f"mix{ch}")
        wraw = m.sb("wraw", [P, 2, KC, P])
        whi, wlo = m.sb("whi", [P, 2, KC, P], F32R), m.sb("wlo", [P, 2, KC, P], F32R)
        tiles = row_tiles(ch, [SUB * s for s in range(NS)])
        xs = m.sb("xs", [P, 2, len(tiles), P])
        sq, acc = m.sb("sq", [P, 2, HALF]), m.sb("acc", [P, HALF])
        gain = m.sb("gain", [P, KC])
        ss, rs, tmp = m.sb("ss", [P, len(EDGES)]), m.sb("rs", [P, len(EDGES)]), m.sb("tmp", [P, len(EDGES)])
        diag = m.sb("diag", [P, len(EDGES), P])
        ps_h, ps_n = m.ps("ps_h", [P, 2, NS, 512]), m.ps("ps_n", [P, 512])
        pair = lambda name: [m.sem(f"{name}{u}") for u in range(2)]
        mixed, mix_hi, mix_lo, gain_loaded = m.sem("mixed"), m.sem("mix_hi"), m.sem("mix_lo"), m.sem("gain_loaded")
        w_loaded, x_loaded, w_lo, product, kept, added = (pair(n) for n in ("w_loaded", "x_loaded", "w_lo", "product", "kept", "added"))
        summed, scaled, spread, normed, n_hi = (m.sem(n) for n in ("summed", "scaled", "spread", "normed", "n_hi"))
        pool_steps, dve_steps = m.sem("pool"), m.sem("dve")
        block = ctx.enter_context(nc.Block())

        @block.sync
        def _(sp):
            for k in range(KC):
                sp.dma_start(nlo[:, k, :].bitcast(F32), t["mixT"][P * k:P * k + P, HALF * ch:HALF * ch + HALF]).then_inc(mixed, 16)
            sp.dma_start(gain[:, :], t["norm2"].rearrange("l (c p) -> p (l c)", p=P), allow_slow_non_contiguous=True).then_inc(gain_loaded, 16)
            def load(i):
                for u in range(2):
                    cols = bass.ds((2 * i + u) * P, P)
                    if not first(i):
                        sp.wait_ge(w_lo[u], i)
                    sp.dma_start(wraw[:, u, :, :], t["w_out"].rearrange("l (c p) n -> p (l c) n", p=P)[:, :, cols]).then_inc(w_loaded[u], 16)
                    if not first(i):
                        sp.wait_ge(product[u], i)
                    for r, (_, w, kind, row) in enumerate(tiles):
                        sp.dma_start(xs[0:w, u, r, :], t[f"x_{kind}"][0, row:row + w, cols]).then_inc(x_loaded[u], 16)

            iterations(sp, load, KC // 2)

        @block.gpsimd
        def _(pool):
            def split(i):
                for u in range(2):
                    pool.wait_ge(w_loaded[u], 16 * (i + 1))
                    if not first(i):
                        pool.wait_ge(product[u], i)
                    one = ones[:, 0:1].unsqueeze(1).broadcast_to([P, KC, P])
                    pool.tensor_tensor(whi[:, u, :, :], wraw[:, u, :, :], one, ALU.mult).then_inc(pool_steps, 1)
                    pool.wait_ge(pool_steps, 2 * i + u + 1)
                    pool.tensor_tensor(wlo[:, u, :, :], wraw[:, u, :, :], whi[:, u, :, :].bitcast(F32), ALU.subtract).then_inc(w_lo[u], 1)

            iterations(pool, split, KC // 2)

        @block.tensor
        def _(pe):
            def columns(i):
                for u in range(2):
                    pe.wait_ge(w_lo[u], i + 1)
                    if not first(i):
                        pe.wait_ge(kept[u], i)
                    for k in range(KC):
                        pe.wait_ge(mix_lo, k + 1)
                        for n, (a, b) in enumerate(((whi, nhi), (whi, nlo), (wlo, nhi))):
                            for s in range(NS):
                                pe.matmul(ps_h[:, u, s, 0:SUB], a[:, u, k, :], b[:, k, SUB * s:SUB * s + SUB], start=(k == 0 and n == 0), stop=False)
                    pe.wait_ge(x_loaded[u], 16 * len(tiles) * (i + 1))
                    for r, (col, w, _, _) in enumerate(tiles):
                        s, o = col // SUB, col % SUB
                        ins = pe.matmul(ps_h[:, u, s, o:o + w], xs[0:w, u, r, :], ident[0:w, 0:w], start=False, stop=(o + w == SUB))
                    ins.then_inc(product[u], 1)

            iterations(pe, columns, KC // 2)
            for u in range(2):
                pe.wait_ge(added[u], KC // 2)
            for j, (lo, hi) in enumerate(EDGES):
                ins = pe.matmul(ps_n[0:hi - lo, j:j + 1], acc[:, lo:hi], ones[:, 0:1], start=True, stop=True)
            ins.then_inc(summed, 1)
            pe.wait_ge(scaled, 1)
            wide = ps_h[:, 0, :, :].rearrange("p s n -> p (s n)")
            for j, (lo, hi) in enumerate(EDGES):
                ins = pe.matmul(wide[:, lo:hi], ones[0:hi - lo, :], diag[0:hi - lo, j, 0:hi - lo], start=True, stop=True)
            ins.then_inc(spread, 1)

        @block.scalar
        def _(act):
            for k in range(KC):
                act.wait_ge(mixed, 16 * KC)
                act.activation(nhi[:, k, :], nlo[:, k, :].bitcast(F32), ACT.Copy).then_inc(mix_hi, 1)

            def keep(i):
                for u in range(2):
                    act.wait_ge(product[u], i + 1)
                    if not first(i):
                        act.wait_ge(added[u], i)
                    src = ps_h[:, u, :, 0:SUB]
                    act.activation(sq[:, u, :].rearrange("p (s n) -> p s n", s=NS), src, ACT.Square)
                    act.activation(hT[:, bass.ds(2 * i + u, 1), :].rearrange("p c (s n) -> p (c s) n", s=NS), src, ACT.Copy).then_inc(kept[u], 1)

            iterations(act, keep, KC // 2)
            for c in range(KC):
                act.wait_ge(normed, c + 1)
                act.activation(nhi[:, c, :], sq[:, c % 2, :], ACT.Copy).then_inc(n_hi, 1)

        @block.vector
        def _(dve):
            st = Steps(dve, dve_steps)
            st.step(dve.memset(acc[:, :], 0.0))
            st.step(dve.memset(ss[:, :], 1.0))
            for k in range(KC):
                dve.wait_ge(mix_hi, k + 1)
                dve.tensor_tensor(nlo[:, k, :], nlo[:, k, :].bitcast(F32), nhi[:, k, :].bitcast(F32), ALU.subtract).then_inc(mix_lo, 1)
            def add(i):
                for u in range(2):
                    dve.wait_ge(kept[u], i + 1)
                    if u:
                        dve.wait_ge(added[0], i + 1)
                    elif not first(i):
                        dve.wait_ge(added[1], i)
                    dve.tensor_tensor(acc[:, :], acc[:, :], sq[:, u, :], ALU.add).then_inc(added[u], 1)

            iterations(dve, add, KC // 2)
            full = HALF // P
            dve.wait_ge(summed, 1)
            dve.tensor_scalar(ss[:, 0:full], ps_n[:, 0:full], 1.0 / D, EPS, ALU.mult, ALU.add)
            rest = HALF - P * full
            st.step(dve.tensor_scalar(ss[0:rest, full:full + 1], ps_n[0:rest, full:full + 1], 1.0 / D, EPS, ALU.mult, ALU.add))
            rsqrt(dve, st, rs[:, :], ss[:, :], tmp[:, :])
            for j in range(len(EDGES)):
                ins = dve.tensor_scalar(diag[:, j, :], ident[:, :], rs[:, j:j + 1], None, ALU.mult)
            ins.then_inc(scaled, 1)
            dve.wait_ge(spread, 1)
            dve.wait_ge(gain_loaded, 16)
            wide = ps_h[:, 0, :, :].rearrange("p s n -> p (s n)")[:, 0:HALF]

            def low(c):
                dve.wait_ge(n_hi, c + 1)
                dve.tensor_tensor(nlo[:, c, :], sq[:, c % 2, :], nhi[:, c, :].bitcast(F32), ALU.subtract).then_inc(mix_lo, 1)
                dve.wait_ge(mix_lo, KC + c + 1)

            for c in range(KC):
                dve.scalar_tensor_tensor(sq[:, c % 2, :], hT[:, c, :], gain[:, c:c + 1], wide, ALU.mult, ALU.mult).then_inc(normed, 1)
                dve.wait_ge(normed, c + 1)
                if c:
                    low(c - 1)
            low(KC - 1)


def phase_feed(nc, t, ch, ident, ones, hT, nhi, nlo, conv, hist):
    with ExitStack() as ctx:
        m = Pool_(nc, ctx, f"ffn{ch}")
        raw_up, raw_down = m.sb("raw_up", [P, 2, KC, 2 * P]), m.sb("raw_down", [P, 2, D])
        up_hi, up_lo = m.sb("up_hi", [P, 4, KC, P], F32R), m.sb("up_lo", [P, 4, KC, P], F32R)
        down_hi, down_lo = m.sb("down_hi", [P, 2, D], F32R), m.sb("down_lo", [P, 2, D], F32R)
        a_hi, a_lo = m.sb("a_hi", [P, 2, HALF], F32R), m.sb("a_lo", [P, 2, HALF], F32R)
        up = m.sb("up", [P, HALF + 4])
        gv = m.sb("gv", [P, 2, HALF])
        idle = m.sb("idle", [P, 2])
        taps = m.sb("taps", [P, 8, 2])
        ps_u, ps_d = m.ps("ps_u", [P, 2, NS, 512]), m.ps("ps_d", [P, 2, 512])
        raw_loaded, down_loaded = [m.sem("raw_loaded0"), m.sem("raw_loaded1")], m.sem("down_loaded")
        up_ready, down_ready, unit_done, based = m.sem("up_ready"), m.sem("down_ready"), m.sem("unit_done"), m.sem("based")
        tap_ready, convolved, gated, a_full, a_high, a_ready = (m.sem(n) for n in ("tap_ready", "convolved", "gated", "a_full", "a_high", "a_ready"))
        partial, partial_read = [m.sem("partial0"), m.sem("partial1")], [m.sem("partial_read0"), m.sem("partial_read1")]
        pool_steps, dve_steps, hist_moved = m.sem("pool"), m.sem("dve"), m.sem("hist_moved")
        y_turned, y_kept, stored = m.sem("y_turned"), m.sem("y_kept"), [m.sem("stored0"), m.sem("stored1")]
        NIT = FT // 2
        runs = [(0, HALF, 2)] if ch == 0 else [(0, PROMPT_1, 2), (PROMPT_1, HALF, 4)]
        out_tiles = row_tiles(ch, [0])

        block = ctx.enter_context(nc.Block())

        @block.sync
        def _(sp):
            def load(it):
                for half in range(2):
                    if not first(it):
                        sp.wait_ge(up_ready, 4 * it - 1 + half)
                    src = t["w_up"].rearrange("l (c p) (h n) -> p (l h) c n", p=P, h=2)[:, half, :, bass.ds(it * (2 * P), 2 * P)]
                    sp.dma_start(raw_up[:, half, :, :], src).then_inc(raw_loaded[half], 16)
                if not first(it):
                    sp.wait_ge(down_ready, it)
                sp.dma_start(raw_down[:, :, :], t["w_down"].rearrange("l (f p) d -> p (l f) d", p=P)[:, bass.ds(it * 2, 2), :]).then_inc(down_loaded, 16)

            iterations(sp, load, NIT)
            for i, (_, w, kind, row) in enumerate(out_tiles):
                sp.wait_ge(y_kept, i + 1)
                sp.dma_start(t[f"y_{kind}"][0, row:row + w, :], gv[0:w, i % 2, 0:D]).then_inc(stored[i % 2], 16)
            sp.wait_ge(stored[0], 16 * ((len(out_tiles) + 1) // 2))
            sp.wait_ge(stored[1], 16 * (len(out_tiles) // 2))

        @block.gpsimd
        def _(pool):
            st = Steps(pool, pool_steps)

            def split(hi, lo, raw, ready):
                st.step(pool.tensor_tensor(hi, raw, ones[:, 0:1].unsqueeze(1).broadcast_to(list(raw.shape)), ALU.mult))
                pool.tensor_tensor(lo, raw, hi.bitcast(F32), ALU.subtract).then_inc(ready, 1)

            def body(it):
                for q in range(4):
                    e, half = q // 2, q % 2
                    pool.wait_ge(raw_loaded[half], 16 * (it + 1))
                    if not first(it):
                        pool.wait_ge(unit_done, 4 * it - 3 + q)
                    split(up_hi[:, q], up_lo[:, q], raw_up[:, half, :, P * e:P * e + P], up_ready)
                pool.wait_ge(down_loaded, 16 * (it + 1))
                if not first(it):
                    for u in range(2):
                        pool.wait_ge(partial[u], it * (KC * NS // 2))
                split(down_hi[:, :, :], down_lo[:, :, :], raw_down[:, :, :], down_ready)

            iterations(pool, body, NIT, steps=st)

        @block.tensor
        def _(pe):
            def unit(it, q):
                half = q % 2
                pe.wait_ge(up_ready, 4 * it + q + 1)
                if not (first(it) and q < 2):
                    pe.wait_ge(based, 4 * it + q - 1)
                for k in range(KC):
                    for n, (a, b) in enumerate(((up_hi, nhi), (up_hi, nlo), (up_lo, nhi))):
                        for s in range(NS):
                            ins = pe.matmul(ps_u[:, half, s, 0:SUB], a[:, q, k, :], b[:, k, SUB * s:SUB * s + SUB],
                                            start=(k == 0 and n == 0), stop=(k == KC - 1 and n == 2))
                ins.then_inc(unit_done, 1)

            def down(it):
                pe.wait_ge(a_ready, 2 * it + 2)
                pe.wait_ge(down_ready, it + 1)
                for j in range(KC * NS):
                    c, s = j // NS, j % NS
                    pe.wait_ge(partial_read[j % 2], it * (KC * NS // 2) + (j // 2 + 1))
                    for e in range(2):
                        for n, (a, b) in enumerate(((down_hi, a_hi), (down_hi, a_lo), (down_lo, a_hi))):
                            ins = pe.matmul(ps_d[:, j % 2, 0:SUB], a[:, e, P * c:P * c + P], b[:, e, SUB * s:SUB * s + SUB],
                                            start=(e == 0 and n == 0), stop=(e == 1 and n == 2))
                    ins.then_inc(partial[j % 2], 1)

            for q in range(4):
                unit(0, q)
            with pe.Fori(1, NIT) as it:
                unit(it, 0)
                down(it - 1)
                for q in range(1, 4):
                    unit(it, q)
            down(NIT - 1)
            for u in range(2):
                pe.wait_ge(partial_read[u], NIT * KC * NS // 2 + 1)
            pe.wait_ge(based, 4 * NIT)
            for i, (col, w, _, _) in enumerate(out_tiles):
                if i >= 2:
                    pe.wait_ge(y_kept, i - 1)
                for c in range(KC):
                    ins = pe.transpose(ps_u[0:w, i % 2, c // 4, P * (c % 4):P * (c % 4) + P], hT[:, c, col:col + w], ident[:, :])
                ins.then_inc(y_turned, 1)

        @block.scalar
        def _(act):
            def body(it):
                act.wait_ge(tap_ready, it + 1)
                for q in range(4):
                    e, half = q // 2, q % 2
                    act.wait_ge(unit_done, 4 * it + q + 1)
                    if not (first(it) and q == 0):
                        act.wait_ge(convolved, 4 * it + q)
                    for lo, hi, shift in runs:
                        whole = hi // SUB if lo == 0 else 0
                        if whole:
                            act.activation(up[:, shift:shift + whole * SUB].rearrange("p (s n) -> p s n", n=SUB), ps_u[:, half, 0:whole, 0:SUB], ACT.Copy)
                        a = max(lo, whole * SUB)
                        if a < hi:
                            act.activation(up[:, a + shift:hi + shift], ps_u[:, half, a // SUB, a % SUB:(hi - 1) % SUB + 1], ACT.Copy)
                    if not (first(it) and q < 2):
                        act.wait_ge(a_ready, 2 * it + e)
                    act.activation(gv[:, half, :].rearrange("p (s n) -> p s n", s=NS), ps_u[:, half, :, 0:SUB], ACT.Identity,
                                   scale=taps[:, 4 + half, e:e + 1], bias=taps[:, 6 + half, e:e + 1]).then_inc(based, 1)
                    act.wait_ge(convolved, 4 * it + q + 1)
                    if half == 0:
                        act.activation(gv[:, 0, :], gv[:, 0, :], ACT.Silu).then_inc(gated, 1)
                    else:
                        act.wait_ge(a_full, 2 * it + e + 1)
                        act.activation(a_hi[:, e, :], gv[:, 1, :], ACT.Copy).then_inc(a_high, 1)

            iterations(act, body, NIT)
            for i, (_, w, _, _) in enumerate(out_tiles):
                act.wait_ge(y_turned, i + 1)
                if i >= 2:
                    act.wait_ge(stored[i % 2], 16 * (i // 2))
                act.activation(gv[0:w, i % 2, 0:D].rearrange("p (s n) -> p s n", s=2), ps_u[0:w, i % 2, 0:2, :], ACT.Copy).then_inc(y_kept, 1)

        @block.vector
        def _(dve):
            st = Steps(dve, dve_steps)
            tails = [(0, HALF + 2)] if ch == 0 else [(0, PROMPT_1 + 2), (1, HALF + 4)]

            def hist_at(which, it, q):
                return hist[which][:, :, bass.ds(it * 2 + (FT * (q % 2) + q // 2), 1)].rearrange("p j f -> p (j f)")

            def body(it):
                dve.tensor_copy(taps[:, :, :], conv[:, :, bass.ds(it * 2, 2)]).then_inc(tap_ready, 1)
                dve.wait_ge(tap_ready, it + 1)
                for q in range(4):
                    e, half = q // 2, q % 2
                    if not (first(it) and q == 0):
                        dve.wait_ge(convolved, 4 * it + q)
                    for which, (lo, _, shift) in enumerate(runs):
                        dve.tensor_copy(up[:, lo + shift - 2:lo + shift], hist_at(which, it, q)).then_inc(hist_moved, 1)
                    dve.wait_ge(hist_moved, len(runs) * (4 * it + q + 1))
                    dve.wait_ge(based, 4 * it + q + 1)
                    for j in (1, 0):
                        for lo, hi, shift in runs:
                            ins = dve.scalar_tensor_tensor(gv[:, half, lo:hi], up[:, lo + shift + j - 2:hi + shift + j - 2], taps[:, 2 * j + half, e:e + 1],
                                                           gv[:, half, lo:hi], ALU.mult, ALU.add)
                            if j:
                                st.step(ins)
                    for which, end in tails:
                        ins = dve.tensor_copy(hist_at(which, it, q), up[:, end - 2:end])
                    ins.then_inc(convolved, 1)
                    if half:
                        dve.wait_ge(gated, 2 * it + e + 1)
                        dve.wait_ge(convolved, 4 * it + q + 1)
                        dve.tensor_tensor(gv[:, 1, :], gv[:, 0, :], gv[:, 1, :], ALU.mult).then_inc(a_full, 1)
                        dve.wait_ge(a_high, 2 * it + e + 1)
                        dve.tensor_tensor(a_lo[:, e, :], gv[:, 1, :], a_hi[:, e, :].bitcast(F32), ALU.subtract).then_inc(a_ready, 1)
                        dve.wait_ge(a_ready, 2 * it + e + 1)
                    if q == 0 and not first(it):
                        add(it - 1)

            def add(it):
                for j in range(KC * NS):
                    c, s = j // NS, j % NS
                    dve.wait_ge(partial[j % 2], it * (KC * NS // 2) + (j // 2 + 1))
                    at = hT[:, c, SUB * s:SUB * s + SUB]
                    dve.tensor_tensor(at, at, ps_d[:, j % 2, 0:SUB], ALU.add).then_inc(partial_read[j % 2], 1)

            for u in range(2):
                dve.memset(idle[:, u:u + 1], 0.0).then_inc(partial_read[u], 1)
            iterations(dve, body, NIT, steps=st)
            add(NIT - 1)


def load_conv(nc, t, ident, ones, conv, hist):
    with ExitStack() as ctx:
        m = Pool_(nc, ctx, "conv")
        FU = 2 * FT
        rows = m.sb("rows", [P, 2, P])
        before = m.sb("before", [2 * FU, P])
        ps = m.ps("ps", [P, 3, 512])
        loaded, turned, done = m.sem("loaded"), m.sem("turned"), m.sem("done")
        block = ctx.enter_context(nc.Block())
        src_w = t["conv_w"].rearrange("l j (f p) -> (l j f) p", p=P)
        src_b = t["conv_b"].rearrange("l (f p) -> (l f) p", p=P)

        @block.sync
        def _(sp):
            sp.dma_start(rows[0:2 * FU, 0, :], src_w[0:2 * FU]).then_inc(loaded, 16)
            sp.dma_start(rows[0:FU, 1, :], src_w[2 * FU:3 * FU]).then_inc(loaded, 16)
            sp.dma_start(rows[FU:2 * FU, 1, :], src_b).then_inc(loaded, 16)
            sp.dma_start(before[:, :], t["state_ffn_conv"].rearrange("l b j (f p) -> (l b j f) p", p=P)).then_inc(loaded, 16)

        @block.tensor
        def _(pe):
            pe.wait_ge(loaded, 64)
            for n in range(3):
                src = before[:, :] if n == 2 else rows[0:2 * FU, n, :]
                pe.transpose(ps[:, n, 0:2 * FU], src, ident[0:2 * FU, 0:2 * FU]).then_inc(turned, 1)

        @block.vector
        def _(dve):
            dve.wait_ge(turned, 3)
            for n in range(2):
                dve.tensor_copy(conv[:, 4 * n:4 * n + 4, :].rearrange("p j f -> p (j f)"), ps[:, n, 0:2 * FU]).then_inc(done, 1)
            dve.tensor_copy(hist[1][:, :, :].rearrange("p j f -> p (j f)"), ps[:, 2, 0:2 * FU]).then_inc(done, 1)
            dve.memset(hist[0][:, :, :], 0.0).then_inc(done, 1)
            dve.memset(ones[:, :], 1.0).then_inc(done, 1)
            dve.wait_ge(done, 5)


def store_conv(nc, t, ident, hist):
    with ExitStack() as ctx:
        m = Pool_(nc, ctx, "tail")
        FU = 2 * FT
        rows = m.sb("rows", [2 * FU, 2, P])
        ps = m.ps("ps", [2 * FU, 2, 512])
        turned, kept, stored = m.sem("turned"), m.sem("kept"), m.sem("stored")
        block = ctx.enter_context(nc.Block())

        @block.tensor
        def _(pe):
            for n in range(2):
                pe.transpose(ps[:, n, 0:P], hist[n][:, :, :].rearrange("p j f -> p (j f)"), ident[:, :]).then_inc(turned, 1)

        @block.vector
        def _(dve):
            dve.wait_ge(turned, 2)
            dve.tensor_copy(rows[:, :, :], ps[:, :, 0:P]).then_inc(kept, 1)

        @block.sync
        def _(sp):
            sp.wait_ge(kept, 1)
            for n, kind in enumerate(("prompt", "sample")):
                sp.dma_start(t[f"new_conv_{kind}"].rearrange("l b j (f p) -> (l b j f) p", p=P), rows[:, n, :]).then_inc(stored, 16)
            sp.wait_ge(stored, 32)


OUTPUTS = (
    ("y_prompt", (1, SEQ, D)), ("y_sample", (1, TS, D)),
    ("new_k_prompt", (1, 1, SEQ, NKV, HD)), ("new_v_prompt", (1, 1, SEQ, NKV, HD)), ("new_kidx_prompt", (1, 1, SEQ, ID)),
    ("new_mem_k_prompt", (1, 1, MT, MH, HD)), ("new_mem_v_prompt", (1, 1, MT, MH, HD)),
    ("new_pool_prompt", (1, 1, HIST, PW)), ("new_conv_prompt", (1, 1, 2, 2 * FF)),
    ("new_k_sample", (1, 1, TS, NKV, HD)), ("new_v_sample", (1, 1, TS, NKV, HD)), ("new_kidx_sample", (1, 1, TS, ID)),
    ("new_pool_sample", (1, 1, HIST, PW)), ("new_conv_sample", (1, 1, 2, 2 * FF)),
)


def program(nc, t):
    t["sT"] = nc.dram_tensor("scratch_sT", (NB + 1, P, NSLOT * P), F32).ap()
    t["mixT"] = nc.dram_tensor("scratch_mixT", (D, ROWS), F32).ap()
    with ExitStack() as ctx:
        ident = ctx.enter_context(nc.sbuf_tensor("ident", [P, P], F32))
        with ExitStack() as attention:
            k = Pool_(nc, attention, "keep")
            keep = {
                "ident": ident,
                "ksT": k.sb("ksT", [P, NKV, LS], F32R), "kisT": k.sb("kisT", [P, LS], F32R),
                "vs": k.sb("vs", [P, 5, NKV * HD]),
                "mkT": k.sb("mkT", [P, 2, MH, MT], F32R),
                "mv": k.sb("mv", [P, 2, 2, MH * HD]),
                "w8": k.sb("w8", [P, NB + 1, IH]),
                "pool_scale": k.sb("pool_scale", [P, 2]),
            }
            phase_memory(nc, t, keep)
            phase_project(nc, t, keep)
            phase_attend(nc, t, keep)
        clear_semaphores(nc)
        f = Pool_(nc, ctx, "feed")
        hT = f.sb("hT", [P, KC, HALF])
        nhi, nlo = f.sb("nhi", [P, KC, HALF], F32R), f.sb("nlo", [P, KC, HALF], F32R)
        ones = f.sb("ones", [P, P])
        conv = f.sb("conv", [P, 8, FT])
        hist = [f.sb(f"hist{n}", [P, 2, 2 * FT]) for n in range(2)]
        load_conv(nc, t, ident, ones, conv, hist)
        for ch in range(2):
            phase_mix(nc, t, ch, ident, ones, hT, nhi, nlo)
            phase_feed(nc, t, ch, ident, ones, hT, nhi, nlo, conv, hist)
        store_conv(nc, t, ident, hist)


def constants():
    f = np.float32
    pos = np.arange(SEQ, dtype=f)[:, None]
    table = []
    for half in (8, 4):
        inv = np.power(f(500000.0), -np.arange(half, dtype=f) / f(half)).astype(f)
        ang = (pos * inv[None]).astype(f).astype(np.float64)
        cos, sin = np.cos(ang).astype(f), np.sin(ang).astype(f)
        table += [cos, cos, -sin, sin]
    s, r = np.arange(P)[:, None], np.arange(P)[None, :]
    band, first, old = [], [], []
    for w in WINDOWS:
        inside = (s <= r) & (s > r - w)
        band.append(inside / f(w) - (s == r))
        first.append(inside / np.minimum(w, r + 1).astype(f) - (s == r))
        old.append(((s - P) > r - w)[96:] / f(w))
    return {"rope_table": np.concatenate(table, 1).astype(f), "band": np.array(band, f), "band_first": np.array(first, f),
            "band_old": np.array(old, f)}


def kernel(**inputs):
    import concourse.bacc as bacc
    from concourse.bass_utils import run_bass_kernel_spmd

    nc = bacc.Bacc("TRN2", target_bir_lowering=False, num_devices=1)
    arrays, t = {}, {}
    for name, a in list(inputs.items()) + list(constants().items()):
        a = np.ascontiguousarray(a)
        arrays[f"in_{name}"] = a
        t[name] = nc.dram_tensor(f"in_{name}", a.shape, mybir.dt.from_np(a.dtype), kind="ExternalInput").ap()
    for name, shape in OUTPUTS:
        t[name] = nc.dram_tensor(f"out_{name}", shape, F32, kind="ExternalOutput").ap()
    program(nc, t)
    r = run_bass_kernel_spmd(nc, [arrays], core_ids=[0])
    return tuple(r.results[0][f"out_{name}"] for name, _ in OUTPUTS)
```

```python
import numpy as np
from contextlib import ExitStack

import concourse.bass as bass
import concourse.mybir as mybir
from concourse.alu_op_type import AluOpType as ALU

F32, F32R, I32 = mybir.dt.float32, mybir.dt.float32r, mybir.dt.int32
ACT = mybir.ActivationFunctionType
AX = mybir.AxisListType

P = 128
D, SEQ, TS, PAST = 1024, 2048, 64, 512
ROWS = SEQ + TS
KC = D // P
NB = SEQ // P
HD, NH, NKV = 64, 8, 2
GQ = NH // NKV
IH, ID = 8, 32
MT, MH = 256, 4
PW, PG, HIST = 256, 4, 15
WINDOWS = (2, 4, 8, 16)
FF = 2816
FT = FF // P
CHUNK = 64
EPS = 1e-6
U0, Q0, K0, V0, QI0, KI0, WI0, QM0, INW = 0, 256, 768, 896, 1024, 1280, 1312, 1320, 1576
GROUPS = ((0, 512), (512, 1024), (1024, 1320), (1320, 1576))
LS = PAST + TS
TOPK_P, TOPK_S = min(256, SEQ // 4), min(256, LS // 4)
SLOT_Q, SLOT_QI, SLOT_QM, SLOT_K, SLOT_KI = 0, 8, 16, 20, 22
NSLOT = 23
MASKED = -1.0e30
HALVINGS = 12
FAR = 1.0e30
UNSEEN, TAKEN, TAKEN_BELOW = -2.0e38, -3.0e38, -2.5e38


class Steps:

    def __init__(self, eng, sem, done=0):
        self.eng, self.sem, self.done = eng, sem, done

    def step(self, instruction):
        instruction.then_inc(self.sem, 1)
        self.done = self.done + 1
        self.eng.wait_ge(self.sem, self.done)


RSQRT_SEED = 1597463007.0


def rsqrt(dve, st, r, v, t, signal=None):
    st.step(dve.tensor_scalar(r.bitcast(I32), v.bitcast(I32), -0.5, RSQRT_SEED, ALU.mult, ALU.add))
    for i in range(4):
        st.step(dve.tensor_tensor(t, r, r, ALU.mult))
        st.step(dve.scalar_tensor_tensor(t, t, -0.5, v, ALU.mult, ALU.mult))
        last = dve.scalar_tensor_tensor(r, t, 1.5, r, ALU.add, ALU.mult)
        if i == 3 and signal is not None:
            last.then_inc(signal, 1)
        else:
            st.step(last)


def flat(ap, pattern):
    return ap.rearrange(pattern)


def squeeze(ap):
    return ap.rearrange("p a n -> p (a n)")


class Pool_:

    def __init__(self, nc, ctx, tag):
        self.nc, self.ctx, self.tag = nc, ctx, tag

    def sb(self, name, shape, dt=F32):
        return self.ctx.enter_context(self.nc.sbuf_tensor(f"{self.tag}_{name}", shape, dt))

    def ps(self, name, shape, dt=F32):
        return self.ctx.enter_context(self.nc.psum_tensor(f"{self.tag}_{name}", shape, dt))

    def sem(self, name):
        return self.ctx.enter_context(self.nc.semaphore(f"{self.tag}_{name}"))


def clear_semaphores(nc):
    with nc.Block() as block:

        @block.gpsimd
        def _(pool):
            used = sorted(nc.released_uncleared_semaphores)
            assert used == list(range(used[0], used[-1] + 1))
            pool.sem_clear(range(used[0], used[-1] + 1))


def phase_memory(nc, t, keep):
    with ExitStack() as ctx:
        m = Pool_(nc, ctx, "mem")
        mem = m.sb("mem", [P, 2, D])
        wraw = m.sb("wraw", [P, KC, 512])
        whi, wlo = m.sb("whi", [P, KC, 512], F32R), m.sb("wlo", [P, KC, 512], F32R)
        gain = m.sb("gain", [P, KC])
        kgain = m.sb("kgain", [P, HD])
        cache_k = m.sb("cache_k", [P, 4, NKV * HD])
        cache_ki = m.sb("cache_ki", [P, 4, ID])
        cache_mk = m.sb("cache_mk", [P, 2, MH * HD])
        junk = m.sb("junk", [P, D])
        ss, rs, tmp = m.sb("ss", [P, 2]), m.sb("rs", [P, 2]), m.sb("tmp", [P, 8])
        ssh, rsh = m.sb("ssh", [P, 8]), m.sb("rsh", [P, 8])
        xhi, xlo = m.sb("xhi", [P, KC, P], F32R), m.sb("xlo", [P, KC, P], F32R)
        kv = m.sb("kv", [P, 2, 512])
        stack = m.sb("stack", [P, 28, P], F32R)
        ps_x, ps_kv, ps_t = m.ps("ps_x", [P, D]), m.ps("ps_kv", [P, 2, 512]), m.ps("ps_t", [P, 2, 512])
        loaded, ident_ready, w_hi, w_lo = m.sem("loaded"), m.sem("ident"), m.sem("w_hi"), m.sem("w_lo")
        squares, xt, x_hi, x_lo, product = m.sem("squares"), m.sem("xt"), m.sem("x_hi"), m.sem("x_lo"), m.sem("product")
        rstd_ready, kv_out, stacked, turned, kept = m.sem("rstd"), m.sem("kv_out"), m.sem("stacked"), m.sem("turned"), m.sem("kept")
        dve_steps, pool_steps, stored = m.sem("dve"), m.sem("pool"), m.sem("stored")
        ident = keep["ident"]
        LOADS = 11
        block = ctx.enter_context(nc.Block())

        @block.sync
        def _(sp):
            loads = [
                (mem[:, :, :], t["mem_prompt"].rearrange("b (m p) d -> p (b m) d", p=P)),
                (wraw[:, :, 0:256], t["w_mem_k"].rearrange("l (c p) n -> p (l c) n", p=P)),
                (wraw[:, :, 256:512], t["w_mem_v"].rearrange("l (c p) n -> p (l c) n", p=P)),
                (gain[:, :], t["mem_norm"].rearrange("l (c p) -> p (l c)", p=P)),
                (kgain[:, :], t["mem_k_norm"].broadcast_to([P, HD])),
                (cache_k[:, :, :], t["cache_k"].rearrange("l b (c p) h d -> p (l b c) (h d)", p=P)),
                (cache_ki[:, :, :], t["cache_kidx"].rearrange("l b (c p) d -> p (l b c) d", p=P)),
                (cache_mk[:, :, :], t["cache_mem_k"].rearrange("l b (c p) h d -> p (l b c) (h d)", p=P)),
                (keep["vs"][:, 0:4, :], t["cache_v"].rearrange("l b (c p) h d -> p (l b c) (h d)", p=P)),
                (keep["mv"][:, 1, :, :], t["cache_mem_v"].rearrange("l b (c p) h d -> p (l b c) (h d)", p=P)),
            ]
            assert len(loads) + 1 == LOADS
            for dst, src in loads:
                sp.dma_start(dst, src, allow_slow_non_contiguous=len(dst.shape) == 2).then_inc(loaded, 16)
            sp.dma_start(keep["pool_scale"][:, :], t["pool_scale"].rearrange("l (c p) -> p (l c)", p=P),
                         allow_slow_non_contiguous=True).then_inc(loaded, 16)
            for i in range(2):
                sp.wait_ge(kv_out, i + 1)
                for n, name in enumerate(("new_mem_k_prompt", "new_mem_v_prompt")):
                    dst = t[name].rearrange("l b (m p) h d -> (l b m) p (h d)", p=P)[i]
                    sp.dma_start(dst, kv[:, i, 256 * n:256 * n + 256]).then_inc(stored, 16)
            sp.wait_ge(stored, 64)

        @block.gpsimd
        def _(pool):
            pool.memset(ident[:, :], 0.0).then_inc(pool_steps, 1)
            pool.wait_ge(pool_steps, 1)
            pool.affine_select(out=ident[:, :], in_=ident[:, :], compare_op=ALU.not_equal, fill=1.0, base=0,
                               pattern=[[-1, P]], channel_multiplier=1).then_inc(ident_ready, 1)

        @block.scalar
        def _(act):
            act.wait_ge(loaded, 16 * LOADS)
            for i in range(2):
                act.activation(junk[:, :], mem[:, i, :], ACT.Square, accum_out=ss[:, i:i + 1]).then_inc(squares, 1)
                act.wait_ge(squares, i + 1)
            for c in range(KC):
                act.activation(whi[:, c, :], wraw[:, c, :], ACT.Identity, scale=gain[:, c:c + 1]).then_inc(w_hi, 1)
            for i in range(2):
                act.wait_ge(xt, i + 1)
                if i:
                    act.wait_ge(product, i)
                for h in range(2):
                    ins = act.activation(xhi[:, 4 * h:4 * h + 4, :], ps_x[:, 512 * h:512 * h + 512].rearrange("p (c n) -> p c n", n=P), ACT.Copy)
                ins.then_inc(x_hi, 1)

        @block.tensor
        def _(pe):
            pe.wait_ge(ident_ready, 1)
            pe.wait_ge(loaded, 16 * LOADS)
            for i in range(2):
                if i:
                    pe.wait_ge(x_lo, i)
                for c in range(KC):
                    ins = pe.transpose(ps_x[:, P * c:P * c + P], mem[:, i, P * c:P * c + P], ident[:, :])
                ins.then_inc(xt, 1)
                pe.wait_ge(x_lo, i + 1)
                pe.wait_ge(w_lo, KC)
                for c in range(KC):
                    for n, (a, b) in enumerate(((xhi, whi), (xhi, wlo), (xlo, whi))):
                        ins = pe.matmul(ps_kv[:, i, :], a[:, c, :], b[:, c, :], start=(c == 0 and n == 0), stop=(c == KC - 1 and n == 2))
                ins.then_inc(product, 1)
            for g in range(7):
                pe.wait_ge(stacked, (1, 2, 3, 4, 5, 5, 6)[g])
                if g >= 2:
                    pe.wait_ge(kept, g - 1)
                for s in range(4):
                    ins = pe.transpose(ps_t[:, g % 2, P * s:P * s + P], stack[:, 4 * g + s, :].bitcast(F32), ident[:, :])
                ins.then_inc(turned, 1)

        @block.vector
        def _(dve):
            st = Steps(dve, dve_steps)
            dve.wait_ge(squares, 2)
            st.step(dve.tensor_scalar(ss[:, :], ss[:, :], 1.0 / D, EPS, ALU.mult, ALU.add))
            rsqrt(dve, st, rs[:, :], ss[:, :], tmp[:, 0:2])
            for c in range(KC):
                dve.wait_ge(w_hi, c + 1)
                dve.scalar_tensor_tensor(wlo[:, c, :], wraw[:, c, :], gain[:, c:c + 1], whi[:, c, :].bitcast(F32),
                                         ALU.mult, ALU.subtract).then_inc(w_lo, 1)
            for i in range(2):
                dve.wait_ge(x_hi, i + 1)
                for h in range(2):
                    ins = dve.tensor_tensor(xlo[:, 4 * h:4 * h + 4, :], ps_x[:, 512 * h:512 * h + 512].rearrange("p (c n) -> p c n", n=P),
                                            xhi[:, 4 * h:4 * h + 4, :].bitcast(F32), ALU.subtract)
                ins.then_inc(x_lo, 1)
            for i in range(2):
                dve.wait_ge(product, i + 1)
                st.step(dve.tensor_scalar(kv[:, i, :], ps_kv[:, i, :], rs[:, i:i + 1], None, ALU.mult))
                keys = kv[:, i, 0:256].rearrange("p (h d) -> p h d", d=HD)
                st.step(dve.tensor_tensor(junk[:, 0:256], kv[:, i, 0:256], kv[:, i, 0:256], ALU.mult))
                st.step(dve.tensor_reduce(ssh[:, 0:4], junk[:, 0:256].rearrange("p (h d) -> p h d", d=HD), AX.X, ALU.add))
                st.step(dve.tensor_scalar(ssh[:, 0:4], ssh[:, 0:4], 1.0 / HD, EPS, ALU.mult, ALU.add))
                rsqrt(dve, st, rsh[:, 0:4], ssh[:, 0:4], tmp[:, 0:4])
                st.step(dve.tensor_tensor(keys, keys, rsh[:, 0:4].unsqueeze(2).broadcast_to([P, 4, HD]), ALU.mult))
                st.step(dve.tensor_tensor(keys, keys, kgain[:, :].unsqueeze(1).broadcast_to([P, 4, HD]), ALU.mult))
                dve.tensor_copy(keep["mv"][:, 0, i, :], kv[:, i, 256:512]).then_inc(kv_out, 1)
                split_rows(dve, st, stack[:, 4 * i:4 * i + 4, :], keys, HD, signal=stacked)
            for i in range(2):
                split_rows(dve, st, stack[:, 8 + 4 * i:12 + 4 * i, :], cache_mk[:, i, :].rearrange("p (h d) -> p h d", d=HD), HD,
                           signal=stacked)
            split_rows(dve, st, stack[:, 16:24, :], cache_k[:, :, :].rearrange("p c (h d) -> p (c h) d", d=HD), HD, signal=stacked)
            split_index(dve, st, stack[:, 24:28, :], cache_ki[:, :, :], key=True, signal=stacked)
            for g in range(7):
                dve.wait_ge(turned, g + 1)
                src = ps_t[:, g % 2, :].rearrange("p (s n) -> p s n", n=P)
                if g < 4:
                    ins = dve.tensor_copy(keep["mkT"][:, g // 2, :, P * (g % 2):P * (g % 2) + P], src)
                elif g < 6:
                    for j in range(NKV):
                        dst = keep["ksT"][:, j, 256 * (g - 4):256 * (g - 4) + 256].rearrange("p (c n) -> p c n", n=P)
                        ins = dve.tensor_copy(dst, ps_t[:, g % 2, :].rearrange("p (c h n) -> p h c n", h=NKV, n=P)[:, j])
                else:
                    ins = dve.tensor_copy(keep["kisT"][:, 0:512], ps_t[:, g % 2, :])
                ins.then_inc(kept, 1)
            dve.wait_ge(kept, 7)


def split_rows(dve, st, out, x, n, signal=None):
    st.step(dve.tensor_copy(out[:, :, 0:n], x))
    last = dve.tensor_tensor(out[:, :, n:2 * n], x, out[:, :, 0:n].bitcast(F32), ALU.subtract)
    if signal is not None:
        last.then_inc(signal, 1)


def split_index(dve, st, out, x, key, signal=None):
    hi, lo = ((0, 2), (1, 3)) if key else ((0, 1), (2, 3))
    part = lambda n: out[:, :, ID * n:ID * n + ID]
    for n in hi:
        first = dve.tensor_copy(part(n), x)
    st.step(first)
    for n in lo:
        last = dve.tensor_tensor(part(n), x, part(hi[0]).bitcast(F32), ALU.subtract)
    if signal is not None:
        last.then_inc(signal, 1)


def phase_project(nc, t, keep):
    with ExitStack() as ctx:
        m = Pool_(nc, ctx, "proj")
        whi, wlo = m.sb("whi", [P, KC, INW], F32R), m.sb("wlo", [P, KC, INW], F32R)
        wraw = m.sb("wraw", [P, 2, INW])
        gain = m.sb("gain", [P, KC])
        hgain = m.sb("hgain", [P, 14, HD])
        x = m.sb("x", [P, 2, D])
        rope = m.sb("rope", [P, 2, 48])
        xhi, xlo = m.sb("xhi", [P, KC, P], F32R), m.sb("xlo", [P, KC, P], F32R)
        pr = m.sb("pr", [P, 2, INW])
        qn = m.sb("qn", [P, 2, 14, HD])
        stack = wraw[:, :, :].rearrange("p a n -> p (a n)")[:, 0:NSLOT * P].rearrange("p (s n) -> p s n", n=P).bitcast(F32R)
        sT = m.sb("sT", [P, NSLOT, P], F32R)
        junk = m.sb("junk", [P, D], mybir.dt.bfloat16)
        rot = m.sb("rot", [P, 2, 10, 16])
        ss, rs, tmp = m.sb("ss", [P, 2]), m.sb("rs", [P, 2]), m.sb("tmp", [P, 16])
        ssh, rsh = m.sb("ssh", [P, 14]), m.sb("rsh", [P, 14])
        u_old, u_old_s = m.sb("u_old", [P, PW]), m.sb("u_old_s", [P, PW])
        band, band0, band_old = m.sb("band", [P, PG, P]), m.sb("band0", [P, PG, P]), m.sb("band_old", [P, PG, P])
        pool_w = m.sb("pool_w", [P, 2, P])
        zT, poolT = m.sb("zT", [P, 2, P]), m.sb("poolT", [P, 2, P])
        ps_x, ps_g, ps_t = m.ps("ps_x", [P, D]), m.ps("ps_g", [P, 4, 512]), m.ps("ps_t", [P, 2, 512])
        consts = m.sem("consts")
        w_loaded, w_hi, w_lo = [m.sem("w_loaded0"), m.sem("w_loaded1")], m.sem("w_hi"), m.sem("w_lo")
        x_loaded = [m.sem("x_loaded0"), m.sem("x_loaded1")]
        rope_loaded = [m.sem("rope_loaded0"), m.sem("rope_loaded1")]
        squares, rstd, xt, x_hi, x_lo = m.sem("squares"), m.sem("rstd"), m.sem("xt"), m.sem("x_hi"), m.sem("x_lo")
        product, product_read, prepared = m.sem("product"), m.sem("product_read"), m.sem("prepared")
        heads_ready, turned, read_act, read_dve = m.sem("heads_ready"), m.sem("turned"), m.sem("read_act"), m.sem("read_dve")
        stored = [m.sem("stored0"), m.sem("stored1")]
        cleared, turned_stored, dve_steps, old_ready, pool_out = m.sem("cleared"), m.sem("turned_stored"), m.sem("dve"), m.sem("old_ready"), m.sem("pool_out")
        ident = keep["ident"]
        NCONST = 12
        STORES = 3
        N_T = 8

        def pipeline(main=None, prepare=None, turn=None, finish=None, loop=None, steps=None):
            stages = [s or (lambda *_: None) for s in (main, prepare, turn, finish)]

            def call(stage, n, u, i):
                stages[stage](n, u, TS if isinstance(n, int) and n == NB else P, i)

            def pair(i):
                for u in range(2):
                    call(0, 2 * i + u + 1, 1 - u, i + u)
                    call(1, 2 * i + u, u, i)
                    call(2, 2 * i + u + 2, u, i + 1)
                    call(3, 2 * i + u, u, i)

            call(2, 0, 0, 0)
            call(0, 0, 0, 0)
            call(2, 1, 1, 0)
            start = steps.done if steps else 0
            pair(0)
            per_pair = steps.done - start if steps else 0
            with loop(1, NB // 2 - 1) as i:
                if steps:
                    steps.done = start + i * per_pair
                pair(i)
            if steps:
                steps.done = start + (NB // 2 - 1) * per_pair
            pair_end = NB // 2 - 1
            n = NB - 2
            call(0, n + 1, 1, pair_end)
            call(1, n, 0, pair_end)
            call(2, n + 2, 0, pair_end + 1)
            call(3, n, 0, pair_end)
            call(0, n + 2, 0, pair_end + 1)
            call(1, n + 1, 1, pair_end)
            call(3, n + 1, 1, pair_end)
            call(1, n + 2, 0, pair_end + 1)
            call(3, n + 2, 0, pair_end + 1)

        def xrows(name_p, name_s, pattern, n, T):
            if T == P:
                return t[name_p].rearrange(pattern, p=P)[bass.ds(n, 1)].rearrange("n p w -> p (n w)")
            return t[name_s].rearrange(pattern, p=TS)[0]

        block = ctx.enter_context(nc.Block())

        @block.sync
        def _(sp):
            sp.wait_ge(cleared, 2)
            for dst, src in (
                (gain[:, :], t["norm1"].rearrange("l (c p) -> p (l c)", p=P)),
                (band[:, :, :], t["band"].rearrange("g p n -> p g n")),
                (band0[:, :, :], t["band_first"].rearrange("g p n -> p g n")),
                (band_old[96:P, :, :], t["band_old"].rearrange("g p n -> p g n")),
                (u_old_s[P - HIST:P, :], t["state_pool"].rearrange("l b r w -> (l b r) w")),
                (hgain[:, 0, :], t["q_norm"].broadcast_to([P, HD])),
                (hgain[:, 8, :], t["k_norm"].broadcast_to([P, HD])),
                (hgain[:, 10, :], t["mem_q_norm"].broadcast_to([P, HD])),
            ):
                sp.dma_start(dst, src, allow_slow_non_contiguous=len(dst.shape) == 2).then_inc(consts, 16)
            for g in range(PG):
                r = HD * (g % 2)
                sp.dma_start(pool_w[r:r + HD, g // 2, r:r + HD], t["pool_w"][0, g]).then_inc(consts, 16)
            for c in range(KC):
                if c >= 2:
                    sp.wait_ge(w_lo, c - 1)
                sp.dma_start(wraw[:, c % 2, :], t["w_in"].rearrange("l (c p) n -> c p (l n)", p=P)[c]).then_inc(w_loaded[c % 2], 16)

            def rows_of(name, n, T, width):
                kind = "prompt" if T == P else "sample"
                flat_rows = t[f"{name}_{kind}"]
                flat_rows = flat_rows.rearrange("l b s d -> (l b s) d") if len(flat_rows.shape) == 4 else flat_rows.rearrange("l b s h d -> (l b s) (h d)")
                return flat_rows[bass.ds(n * P, P)] if T == P else flat_rows

            def store_rows(n, u, T, i):
                sp.wait_ge(heads_ready, n + 1)
                sp.dma_start(rows_of("new_k", n, T, 128), qn[0:T, u, 8:10, :].rearrange("p h d -> p (h d)")).then_inc(stored[u], 16)
                sp.dma_start(rows_of("new_v", n, T, 128), pr[0:T, u, V0:QI0]).then_inc(stored[u], 16)
                sp.dma_start(rows_of("new_kidx", n, T, ID), pr[0:T, u, KI0:WI0]).then_inc(stored[u], 16)

            def store_turned(n, u, T, i):
                sp.wait_ge(read_act, 4 * n + 4)
                sp.wait_ge(read_dve, 4 * n + 4)
                sp.dma_start(t["sT"][bass.ds(n, 1)].rearrange("n p (s w) -> p (n s) w", w=P)[:, :, 0:T], sT[:, :, 0:T].bitcast(F32)).then_inc(turned_stored, 16)
                at = bass.ds(n * P, P) if T == P else slice(SEQ, ROWS)
                sp.dma_start(t["mixT"][0:PW, at].rearrange("(c p) n -> p c n", p=P), poolT[:, :, 0:T]).then_inc(turned_stored, 16)
                if isinstance(n, int) and n >= NB - 1:
                    name = "new_pool_prompt" if T == P else "new_pool_sample"
                    sp.dma_start(t[name].rearrange("l b r w -> (l b r) w"), pr[T - HIST:T, u, U0:Q0]).then_inc(pool_out, 16)

            pipeline(prepare=store_rows, finish=store_turned, loop=sp.Fori)
            sp.wait_ge(stored[0], 16 * STORES * (NB // 2 + 1))
            sp.wait_ge(stored[1], 16 * STORES * (NB // 2))
            sp.wait_ge(turned_stored, 32 * (NB + 1))
            sp.wait_ge(pool_out, 32)

        @block.gpsimd
        def _(pool):
            pool.memset(pool_w[:, :, :], 0.0).then_inc(cleared, 1)
            pool.memset(u_old_s[:, :], 0.0).then_inc(cleared, 1)

            def load(n, u, T, i, first=False):
                if not first:
                    pool.wait_ge(xt, n - 1)
                    pool.wait_ge(squares, n - 1)
                pool.dma_start(x[0:T, u, :], xrows("x_prompt", "x_sample", "b (n p) d -> (b n) p d", n, T)).then_inc(x_loaded[u], 16)
                if not first:
                    pool.wait_ge(prepared, n - 1)
                if T == P:
                    src = t["rope_table"][0:SEQ].rearrange("(n p) w -> n p w", p=P)[bass.ds(n, 1)].rearrange("n p w -> p (n w)")
                else:
                    src = t["rope_table"][PAST:LS]
                pool.dma_start(rope[0:T, u, :], src).then_inc(rope_loaded[u], 16)

            load(0, 0, P, 0, first=True)
            load(1, 1, P, 0, first=True)
            with pool.Fori(1, NB // 2) as i:
                for u in range(2):
                    load(2 * i + u, u, P, i)
            load(NB, 0, TS, 0)

        @block.scalar
        def _(act):
            act.wait_ge(consts, 16 * NCONST)
            for c in range(KC):
                act.wait_ge(w_loaded[c % 2], 16 * (c // 2 + 1))
                act.activation(whi[:, c, :], wraw[:, c % 2, :], ACT.Identity, scale=gain[:, c:c + 1]).then_inc(w_hi, 1)

            def turn(n, u, T, i):
                act.wait_ge(x_loaded[u], 16 * (i + 1))
                act.wait_ge(squares, n)
                act.activation(junk[0:T, :], x[0:T, u, :], ACT.Square, accum_out=ss[0:T, u:u + 1]).then_inc(squares, 1)
                act.wait_ge(xt, n + 1)
                for h in range(2):
                    ins = act.activation(xhi[:, 4 * h:4 * h + 4, 0:T], ps_x[:, 512 * h:512 * h + 512].rearrange("p (c n) -> p c n", n=P)[:, :, 0:T], ACT.Copy)
                ins.then_inc(x_hi, 1)

            def scale(n, u, T, i):
                act.wait_ge(rstd, n + 1)
                if not (isinstance(n, int) and n < 2):
                    act.wait_ge(stored[u], 16 * STORES * i)
                    act.wait_ge(turned, N_T * (n - 1))
                    act.wait_ge(old_ready, n)
                for g, (a, b) in enumerate(GROUPS):
                    act.wait_ge(product, 4 * n + g + 1)
                    act.activation(pr[0:T, u, a:b], ps_g[0:T, g, 0:b - a], ACT.Identity, scale=rs[0:T, u:u + 1]).then_inc(product_read, 1)

            def place(n, u, T, i):
                act.wait_ge(turned_stored, 32 * n)
                for g in (0, 2, 4):
                    act.wait_ge(turned, N_T * n + g + 1)
                    src = ps_t[:, 0, :].rearrange("p (s n) -> p s n", n=P)[:, :, 0:T]
                    act.activation(sT[:, 4 * g:4 * g + 4, 0:T], src, ACT.Copy).then_inc(read_act, 1)
                act.wait_ge(turned, N_T * n + 7)
                act.activation(zT[:, :, 0:T], ps_t[:, 0, 0:256].rearrange("p (s n) -> p s n", n=P)[:, :, 0:T], ACT.Copy).then_inc(read_act, 1)

            pipeline(main=scale, turn=turn, finish=place, loop=act.Fori)

        @block.tensor
        def _(pe):
            pe.wait_ge(consts, 16 * NCONST)

            def turn(n, u, T, i):
                pe.wait_ge(x_loaded[u], 16 * (i + 1))
                pe.wait_ge(x_lo, n)
                for c in range(KC):
                    ins = pe.transpose(ps_x[:, P * c:P * c + T], x[0:T, u, P * c:P * c + P], ident[0:T, 0:T])
                ins.then_inc(xt, 1)

            def product_of(n, u, T, i):
                pe.wait_ge(x_lo, n + 1)
                if isinstance(n, int) and n == 0:
                    pe.wait_ge(w_lo, KC)
                for g, (a, b) in enumerate(GROUPS):
                    if not (isinstance(n, int) and n == 0):
                        pe.wait_ge(product_read, 4 * (n - 1) + g + 1)
                    for c in range(KC):
                        for k, (p, q) in enumerate(((xhi, whi), (xhi, wlo), (xlo, whi))):
                            ins = pe.matmul(ps_g[0:T, g, 0:b - a], p[:, c, 0:T], q[:, c, a:b], start=(c == 0 and k == 0), stop=(c == KC - 1 and k == 2))
                    ins.then_inc(product, 1)

            def turn_stack(n, u, T, i):
                pe.wait_ge(prepared, n + 1)
                for g in range(6):
                    if g >= 2:
                        pe.wait_ge((read_act, read_dve)[g % 2], 4 * n + g // 2)
                    else:
                        pe.wait_ge((read_act, read_dve)[g % 2], 4 * n)
                    for s in range(min(4, NSLOT - 4 * g)):
                        ins = pe.transpose(ps_t[:, g % 2, P * s:P * s + T], stack[0:T, 4 * g + s, :].bitcast(F32), ident[0:T, 0:T])
                    ins.then_inc(turned, 1)
                pe.wait_ge(read_act, 4 * n + 3)
                pe.wait_ge(old_ready, n + 1)
                first = isinstance(n, int) and n == 0
                old = u_old_s if T == TS else u_old
                for g in range(PG):
                    out = ps_t[HD * (g % 2):HD * (g % 2) + HD, 0, P * (g // 2):P * (g // 2) + T]
                    pe.matmul(out, pr[0:T, u, HD * g:HD * g + HD], (band0 if first else band)[0:T, g, 0:T], start=True, stop=False)
                    ins = pe.matmul(out, old[96:P, HD * g:HD * g + HD], band_old[96:P, g, 0:T], start=False, stop=True)
                ins.then_inc(turned, 1)
                pe.wait_ge(read_act, 4 * n + 4)
                pe.wait_ge(read_dve, 4 * n + 3)
                for c in range(2):
                    ins = pe.matmul(ps_t[:, 1, P * c:P * c + T], pool_w[:, c, :], zT[:, c, 0:T], start=True, stop=True)
                ins.then_inc(turned, 1)

            pipeline(main=product_of, turn=turn, finish=turn_stack, loop=pe.Fori)

        @block.vector
        def _(dve):
            st = Steps(dve, dve_steps)
            dve.wait_ge(consts, 16 * NCONST)
            st.step(dve.memset(u_old[:, :], 0.0))
            dve.memset(tmp[:, :], 0.0).then_inc(old_ready, 1)
            st.step(dve.tensor_scalar(hgain[:, 0, :], hgain[:, 0, :], HD ** -0.5, None, ALU.mult))
            st.step(dve.tensor_scalar(hgain[:, 10, :], hgain[:, 10, :], HD ** -0.5, None, ALU.mult))
            for a, b in ((0, 8), (8, 10), (10, 14)):
                st.step(dve.tensor_copy(hgain[:, a + 1:b, :], hgain[:, a:a + 1, :].broadcast_to([P, b - a - 1, HD])))
            for c in range(KC):
                dve.wait_ge(w_hi, c + 1)
                dve.scalar_tensor_tensor(wlo[:, c, :], wraw[:, c % 2, :], gain[:, c:c + 1], whi[:, c, :].bitcast(F32),
                                         ALU.mult, ALU.subtract).then_inc(w_lo, 1)

            def turn(n, u, T, i):
                dve.wait_ge(squares, n + 1)
                st.step(dve.tensor_scalar(ss[0:T, u:u + 1], ss[0:T, u:u + 1], 1.0 / D, EPS, ALU.mult, ALU.add))
                rsqrt(dve, st, rs[0:T, u:u + 1], ss[0:T, u:u + 1], tmp[0:T, 0:1], signal=rstd)
                dve.wait_ge(x_hi, n + 1)
                for h in range(2):
                    ins = dve.tensor_tensor(xlo[:, 4 * h:4 * h + 4, 0:T], ps_x[:, 512 * h:512 * h + 512].rearrange("p (c n) -> p c n", n=P)[:, :, 0:T],
                                            xhi[:, 4 * h:4 * h + 4, 0:T].bitcast(F32), ALU.subtract)
                ins.then_inc(x_lo, 1)

            def rotate(x1, x2, both, cos, sin, w):
                T, heads, half = x1.shape
                a, b = rot[0:T, 0, 0:heads, 0:2 * half], rot[0:T, 1, 0:heads, 0:2 * half]
                dve.tensor_tensor(a, both, cos.unsqueeze(1).broadcast_to([T, heads, 2 * half]), ALU.mult)
                dve.tensor_tensor(b[:, :, 0:half], x2, sin[:, 0:half].unsqueeze(1).broadcast_to([T, heads, half]), ALU.mult)
                st.step(dve.tensor_tensor(b[:, :, half:], x1, sin[:, half:].unsqueeze(1).broadcast_to([T, heads, half]), ALU.mult))
                last = dve.tensor_tensor(both, a, b, ALU.add)
                st.step(last)

            def prepare(n, u, T, i):
                row = pr[0:T, u, :]
                heads = qn[0:T, u, :, :]
                dve.wait_ge(product_read, 4 * n + 4)
                if not (isinstance(n, int) and n < 2):
                    dve.wait_ge(stored[u], 16 * STORES * i)
                ki_row = row[:, KI0:WI0]
                square = heads.rearrange("p h d -> p (h d)")
                dve.tensor_tensor(square[:, 0:640], row[:, Q0:V0], row[:, Q0:V0], ALU.mult)
                st.step(dve.tensor_tensor(square[:, 640:896], row[:, QM0:INW], row[:, QM0:INW], ALU.mult))
                st.step(dve.tensor_reduce(ssh[0:T, :], heads, AX.X, ALU.add))
                st.step(dve.tensor_scalar(ssh[0:T, :], ssh[0:T, :], 1.0 / HD, EPS, ALU.mult, ALU.add))
                rsqrt(dve, st, rsh[0:T, :], ssh[0:T, :], tmp[0:T, 0:14])
                dve.tensor_tensor(heads[:, 0:10, :], row[:, Q0:V0].rearrange("p (h d) -> p h d", d=HD),
                                  rsh[0:T, 0:10].unsqueeze(2).broadcast_to([T, 10, HD]), ALU.mult)
                st.step(dve.tensor_tensor(heads[:, 10:14, :], row[:, QM0:INW].rearrange("p (h d) -> p h d", d=HD),
                                          rsh[0:T, 10:14].unsqueeze(2).broadcast_to([T, 4, HD]), ALU.mult))
                st.step(dve.tensor_tensor(heads, heads, hgain[0:T, :, :], ALU.mult))
                dve.wait_ge(rope_loaded[u], 16 * (i + 1))
                rotate(heads[:, 0:10, 0:8], heads[:, 0:10, 8:16], heads[:, 0:10, 0:16], rope[0:T, u, 0:16], rope[0:T, u, 16:32], 16)
                qi = row[:, QI0:WI0].rearrange("p (h d) -> p h d", d=ID)
                rotate(qi[:, :, 0:4], qi[:, :, 4:8], qi[:, :, 0:8], rope[0:T, u, 32:40], rope[0:T, u, 40:48], 8)
                w_at = keep["w8"][0:T, bass.ds(n, 1), :].rearrange("p n h -> p (n h)")
                dve.tensor_scalar(w_at, row[:, WI0:QM0], (IH * ID) ** -0.5, None, ALU.mult).then_inc(heads_ready, 1)
                split_rows(dve, st, stack[0:T, SLOT_Q:SLOT_Q + 8, :], heads[:, 0:8, :], HD)
                split_rows(dve, st, stack[0:T, SLOT_K:SLOT_K + 2, :], heads[:, 8:10, :], HD)
                split_rows(dve, st, stack[0:T, SLOT_QM:SLOT_QM + 4, :], heads[:, 10:14, :], HD)
                split_index(dve, st, stack[0:T, SLOT_QI:SLOT_QI + 8, :], qi[:, 0:8, :], key=False)
                split_index(dve, st, stack[0:T, SLOT_KI:SLOT_KI + 1, :], qi[:, 8:9, :], key=True, signal=prepared)

            def place(n, u, T, i):
                dve.wait_ge(turned_stored, 32 * n)
                src = ps_t[:, 1, :].rearrange("p (s n) -> p s n", n=P)[:, :, 0:T]
                for g in (1, 3, 5):
                    k = min(4, NSLOT - 4 * g)
                    dve.wait_ge(turned, N_T * n + g + 1)
                    dve.tensor_copy(sT[:, 4 * g:4 * g + k, 0:T], src[:, 0:k, :]).then_inc(read_dve, 1)
                dve.wait_ge(turned, N_T * n + 8)
                for c in range(2):
                    ins = dve.tensor_scalar(poolT[:, c, 0:T], src[:, c, :], keep["pool_scale"][:, c:c + 1], None, ALU.mult)
                ins.then_inc(read_dve, 1)
                if T == P:
                    dve.tensor_copy(u_old[96:P, :], pr[96:P, u, U0:Q0]).then_inc(old_ready, 1)

            pipeline(prepare=prepare, turn=turn, finish=place, loop=dve.Fori, steps=st)



def segments(width):
    count = -(-width // 512)
    size = -(-width // count)
    size += size % 2
    return [(a, min(a + size, width)) for a in range(0, width, size)]


class Rows:

    def __init__(self, n):
        self.n, self.sample = n, n == NB
        self.T = TS if self.sample else P
        self.S = LS if self.sample else P * (n + 1)
        self.segs = segments(self.S)
        self.tiles = [(a, min(a + P, self.S)) for a in range(0, self.S, P)]
        self.keep = TOPK_S if self.sample else (TOPK_P if self.S > TOPK_P else 0)
        self.groups = [self.tiles[a:a + 4] for a in range(0, len(self.tiles), 4)]
        self.at = SEQ if self.sample else P * n


BLOCKS = [Rows(n) for n in range(NB + 1)]


def phase_attend(nc, t, keep):
    with ExitStack() as ctx:
        m = Pool_(nc, ctx, "att")
        kT, kiT = m.sb("kT", [P, NKV, SEQ], F32R), m.sb("kiT", [P, SEQ], F32R)
        v = m.sb("v", [P, NB, NKV * HD])
        qi = m.sb("qi", [P, 2, IH, P], F32R)
        qa = m.sb("qa", [P, 2, 12, P], F32R)
        qb = m.sb("qb", [P, 2, 12, P], F32R)
        diag = m.sb("diag", [P, 2, IH, P])
        relu = m.sb("relu", [P, 3, 512])
        scores, work = m.sb("scores", [P, 2, SEQ]), m.sb("work", [P, SEQ])
        mask = m.sb("mask", [P, 2, SEQ])
        probs = m.sb("probs", [P, 2, SEQ])
        pT = m.sb("pT", [P, 2, NB, P])
        top, idle = m.sb("top", [P, 8]), m.sb("idle", [P, 1])
        mids, counts, steps = m.sb("mids", [P, HALVINGS + 1]), m.sb("counts", [P, HALVINGS + 1]), m.sb("steps", [P, HALVINGS])
        halves, places = m.sb("halves", [P, HALVINGS]), m.sb("places", [P, 16])
        falling, lowest, chosen = m.sb("falling", [P, SEQ]), m.sb("lowest", [P, 16]), m.sb("chosen", [P, 16])
        missing, last_tie = m.sb("missing", [P, 1]), m.sb("last_tie", [P, 1])
        far, low, spread, back = m.sb("far", [P, HALVINGS + 1]), m.sb("low", [P, 1]), m.sb("spread", [P, 1]), m.sb("back", [P, 1])
        bound, above, place, kth = m.sb("bound", [P, 1]), m.sb("above", [P, 1]), m.sb("place", [P, 1]), m.sb("kth", [P, 1])
        reached, split_tie, crowded = m.sb("reached", [P, 1]), m.sb("split_tie", [P, 1]), m.sb("crowded", [P, 1])
        failed, failedT, failures = m.sb("failed", [P, 32]), m.sb("failedT", [P, 32]), m.sb("failures", [P, 1], I32)
        peaks, neg = m.sb("peaks", [P, 2, 4]), m.sb("neg", [P, 2, 12])
        sums, inv = m.sb("sums", [P, 2, 12]), m.sb("inv", [P, 2, 12])
        rows = m.sb("rows", [P, 768])
        rowsT = m.sb("rowsT", [P, 6, P])
        ps_i, ps_s, ps_l = m.ps("ps_i", [P, 2, 512]), m.ps("ps_s", [P, 512]), m.ps("ps_l", [P, 2, 512])
        ps_p, ps_o = m.ps("ps_p", [P, 2, 512]), m.ps("ps_o", [P, 512])
        keys_loaded, q_loaded = m.sem("keys_loaded"), [m.sem("q_loaded0"), m.sem("q_loaded1")]
        qi_loaded = [m.sem("qi_loaded0"), m.sem("qi_loaded1")]
        diag_ready, raw_scores, relu_ready = m.sem("diag_ready"), m.sem("raw_scores"), m.sem("relu_ready")
        seg_summed, seg_kept, scores_taken = m.sem("seg_summed"), m.sem("seg_kept"), m.sem("scores_taken")
        logits, masked, neg_ready, exp_done = m.sem("logits"), m.sem("masked"), m.sem("neg_ready"), m.sem("exp_done")
        turned, copied, pv_done, rows_ready = m.sem("turned"), [m.sem("copied0"), m.sem("copied1")], m.sem("pv_done"), m.sem("rows_ready")
        stored, dve_steps, tie_steps, general_steps = m.sem("stored"), m.sem("dve"), m.sem("ties"), m.sem("general")
        ident = keep["ident"]
        KEY_LOADS, Q_LOADS = 10, 6
        NHEADS = NH + 1

        segs_before, groups_before = [0], [0]
        for b in BLOCKS:
            segs_before.append(segs_before[-1] + len(b.segs))
            groups_before.append(groups_before[-1] + NH * len(b.groups) + 4)

        def group_index(b, h, g):
            return groups_before[b.n] + (h * len(b.groups) + g if h <= NH else NH * len(b.groups) + 2 + g)

        def bank_reads(index):
            return index % 2, index // 2 + 1

        def last_group(seq):
            b, h = BLOCKS[seq // NHEADS], seq % NHEADS
            return group_index(b, h, (len(b.groups) if h < NH else 2) - 1)

        def slots():
            for b in BLOCKS:
                for h in range(NHEADS):
                    yield b, h, (b, h + 1) if h + 1 < NHEADS else (None if b.sample else (BLOCKS[b.n + 1], 0))

        def ahead(b, by):
            return BLOCKS[b.n + by] if b.n + by <= NB else None

        def portion(b, part):
            total = IH * len(b.segs)
            cut = lambda part: total if part == NHEADS else total * part // 12
            return range(cut(part), cut(part + 1))

        def logit_count(b, h, s):
            return NH * segs_before[b.n] + b.n + h * len(b.segs) + s

        def copy_groups(act, b, h):
            count = len(b.groups) if h < NH else 2
            for g in range(count):
                index = group_index(b, h, g)
                e = index % 2
                act.wait_ge(turned, index + 1)
                if h == 9:
                    tiles, dst = (4, 2)[g], rowsT[:, 4 * g:4 * g + (4, 2)[g], 0:b.T]
                    if b.n:
                        act.wait_ge(stored, 16 * b.n)
                    pieces = [(P, dst, ps_p[:, e, 0:P * tiles])]
                else:
                    seq = NHEADS * b.n + h
                    if seq >= 2:
                        act.wait_ge(pv_done, seq - 1)
                    tiles = b.groups[g] if h < NH else [(0, P)] * 4
                    full = sum(hi - lo == P for lo, hi in tiles)
                    pieces = [(P, pT[:, seq % 2, 4 * g:4 * g + full, 0:b.T], ps_p[:, e, 0:P * full])] if full else []
                    if full < len(tiles):
                        w = tiles[-1][1] - tiles[-1][0]
                        pieces.append((w, pT[0:w, seq % 2, 4 * g + full:4 * g + full + 1, 0:b.T], ps_p[0:w, e, P * full:P * full + P]))
                for w, dst, src in pieces:
                    src = src.rearrange("p (s n) -> p s n", n=P)[:, :, 0:b.T]
                    ins = act.activation(dst, src, ACT.Copy)
                ins.then_inc(copied[e], 1)

        block = ctx.enter_context(nc.Block())

        @block.sync
        def _(sp):
            sT = t["sT"].rearrange("n p (s w) -> s p n w", w=P)
            for n in range(2):
                sp.dma_start(qi[:, n, :, :].bitcast(F32), t["sT"][n].rearrange("p (s w) -> p s w", w=P)[:, SLOT_QI:SLOT_QI + IH, :]).then_inc(qi_loaded[n], 16)
            for j in range(NKV):
                sp.dma_start(kT[:, j, :].rearrange("p (n w) -> p n w", w=P).bitcast(F32), sT[SLOT_K + j, :, 0:NB]).then_inc(keys_loaded, 16)
            sp.dma_start(kiT[:, :].rearrange("p (n w) -> p n w", w=P).bitcast(F32), sT[SLOT_KI, :, 0:NB]).then_inc(keys_loaded, 16)
            last = t["sT"][NB].rearrange("p (s w) -> p s w", w=P)
            sp.dma_start(keep["ksT"][:, :, PAST:LS].bitcast(F32), last[:, SLOT_K:SLOT_KI, 0:TS]).then_inc(keys_loaded, 16)
            sp.dma_start(keep["kisT"][:, PAST:LS].bitcast(F32), last[:, SLOT_KI, 0:TS]).then_inc(keys_loaded, 16)
            sp.dma_start(v[:, :, :], t["new_v_prompt"].rearrange("l b (n p) h d -> p (l b n) (h d)", p=P)).then_inc(keys_loaded, 16)
            sp.dma_start(keep["vs"][0:TS, 4, :], t["new_v_sample"].rearrange("l b s h d -> (l b s) (h d)")).then_inc(keys_loaded, 16)

            sp.dma_start(halves[:, :], t["halves"]).then_inc(keys_loaded, 16)
            sp.dma_start(places[:, :], t["places"]).then_inc(keys_loaded, 16)
            sp.dma_start(falling[:, :], t["falling"].broadcast_to([P, SEQ])).then_inc(keys_loaded, 16)

            def load_index(n):
                if n > NB:
                    return
                b, u = BLOCKS[n], n % 2
                if n >= 2:
                    sp.wait_ge(seg_summed, segs_before[n - 1])
                src = t["sT"][n].rearrange("p (s w) -> p s w", w=P)
                sp.dma_start(qi[:, u, :, 0:b.T].bitcast(F32), src[:, SLOT_QI:SLOT_QI + IH, 0:b.T]).then_inc(qi_loaded[u], 16)

            def load(b):
                u = b.n % 2
                if b.n >= 2:
                    sp.wait_ge(pv_done, NHEADS * (b.n - 1))
                src = t["sT"][b.n].rearrange("p (s w) -> p s w", w=P)
                for a, slot, count in ((0, SLOT_Q, 8), (8, SLOT_QM, 4)):
                    sp.dma_start(qa[:, u, a:a + count, 0:b.T].bitcast(F32), src[:, slot:slot + count, 0:b.T]).then_inc(q_loaded[u], 16)
                    for lo, hi in ((0, HD), (HD, P)):
                        sp.dma_start(qb[lo:hi, u, a:a + count, 0:b.T].bitcast(F32), src[P - hi:P - lo, slot:slot + count, 0:b.T]).then_inc(q_loaded[u], 16)

            load(BLOCKS[0])
            load(BLOCKS[1])
            load_index(2)
            load_index(3)
            for b in BLOCKS:
                load_index(b.n + 4)
                for g in range(2):
                    e, count = bank_reads(group_index(b, 9, g))
                    sp.wait_ge(copied[e], count)
                sp.dma_start(t["mixT"][PW:D, b.at:b.at + b.T].rearrange("(c p) n -> p c n", p=P), rowsT[:, :, 0:b.T]).then_inc(stored, 16)
                if b.n + 2 <= NB:
                    load(BLOCKS[b.n + 2])
            sp.wait_ge(stored, 16 * len(BLOCKS))

        @block.gpsimd
        def _(pool):
            for b in BLOCKS:
                if b.n >= 2:
                    pool.wait_ge(seg_summed, segs_before[b.n - 1])
                for h in range(IH):
                    ins = pool.tensor_scalar(diag[0:b.T, b.n % 2, h, 0:b.T], ident[0:b.T, 0:b.T], keep["w8"][0:b.T, b.n, h:h + 1], None, ALU.mult)
                ins.then_inc(diag_ready, 1)

        @block.tensor
        def _(pe):
            def raw_index(b, i):
                if i == 0:
                    pe.wait_ge(qi_loaded[b.n % 2], 16 * (b.n // 2 + 1))
                    pe.wait_ge(diag_ready, b.n + 1)
                lo, hi = b.segs[i // IH]
                count = IH * segs_before[b.n] + i
                if count >= 2:
                    pe.wait_ge(relu_ready, count - 1)
                keys = keep["kisT"] if b.sample else kiT
                pe.matmul(ps_i[0:b.T, count % 2, 0:hi - lo], qi[:, b.n % 2, i % IH, 0:b.T], keys[:, lo:hi],
                          start=True, stop=True).then_inc(raw_scores, 1)

            def index_pieces(b, numbers):
                for i in numbers:
                    if i == 0:
                        raw_index(b, 0)
                    if i + 1 < IH * len(b.segs):
                        raw_index(b, i + 1)
                    h, count = i % IH, IH * segs_before[b.n] + i
                    lo, hi = b.segs[i // IH]
                    if h == 0:
                        pe.wait_ge(seg_kept, segs_before[b.n] + i // IH)
                    pe.wait_ge(relu_ready, count + 1)
                    ins = pe.matmul(ps_s[0:b.T, 0:hi - lo], diag[0:b.T, b.n % 2, h, 0:b.T], relu[0:b.T, count % 3, 0:hi - lo],
                                    start=(h == 0), stop=(h == IH - 1))
                    if h == IH - 1:
                        ins.then_inc(seg_summed, 1)

            def head_logits(b, h, other=None, numbers=range(0)):
                u, T = b.n % 2, b.T
                if h == 0:
                    pe.wait_ge(q_loaded[u], 16 * Q_LOADS * (b.n // 2 + 1))
                if h == NH:
                    pe.wait_ge(masked, logit_count(b, NH, 0))
                    for mh in range(MH):
                        out = ps_l[0:T, mh // 2, 256 * (mh % 2):256 * (mh % 2) + 256]
                        keys = keep["mkT"][:, 1 if b.sample else 0, mh, :]
                        pe.matmul(out, qa[:, u, 8 + mh, 0:T], keys, start=True, stop=False)
                        ins = pe.matmul(out, qb[:, u, 8 + mh, 0:T], keys, start=False, stop=True)
                    ins.then_inc(logits, 1)
                    index_pieces(other, numbers)
                    return
                keys = keep["ksT"] if b.sample else kT
                for s, (lo, hi) in enumerate(b.segs):
                    n = logit_count(b, h, s)
                    if n >= 2:
                        pe.wait_ge(masked, n - 1)
                    if h == 0 and s < 2 and b.n:
                        pe.wait_ge(exp_done, NHEADS * b.n)
                    out = ps_l[0:T, n % 2, 0:hi - lo]
                    pe.matmul(out, qa[:, u, h, 0:T], keys[:, h // GQ, lo:hi], start=True, stop=False)
                    pe.matmul(out, qb[:, u, h, 0:T], keys[:, h // GQ, lo:hi], start=False, stop=True).then_inc(logits, 1)
                    if s >= 1 and s + 1 < len(b.segs):
                        index_pieces(other, numbers[0:2])
                        numbers = numbers[2:]
                index_pieces(other, numbers)

            def turn_group(index, pieces, T):
                e, count = bank_reads(index)
                if count > 1:
                    pe.wait_ge(copied[e], count - 1)
                for i, (src, width) in enumerate(pieces):
                    ins = pe.transpose(ps_p[0:width, e, P * i:P * i + T], src, ident[0:T, 0:T])
                ins.then_inc(turned, 1)

            def head_values(b, h):
                u, T = b.n % 2, b.T
                seq = NHEADS * b.n + h
                pe.wait_ge(exp_done, seq + 1)
                if h < NH:
                    groups, src = b.groups, probs[0:T, seq % 2, :]
                else:
                    groups = [[(P * i, P * i + P) for i in range(4 * g, 4 * g + 4)] for g in range(2)]
                    src = probs[0:T, seq % 2, :]

                def turn(g):
                    turn_group(group_index(b, h, g), [(src[:, lo:hi], hi - lo) for lo, hi in groups[g]], T)

                def multiply(g):
                    e, count = bank_reads(group_index(b, h, g))
                    pe.wait_ge(copied[e], count)
                    if g == 0 and h % GQ == 0:
                        pe.wait_ge(rows_ready, 3 * b.n + h // GQ)
                    for i, (lo, hi) in enumerate(groups[g]):
                        k = 4 * g + i
                        if h < NH:
                            values = (keep["vs"] if b.sample else v)[0:hi - lo, k, :]
                            slot, first, last = h % GQ, k == 0, k == len(b.tiles) - 1
                        else:
                            slot, tile = k // 2, k % 2
                            values = keep["mv"][:, 1 if b.sample else 0, tile, P * (slot // 2):P * (slot // 2) + P]
                            first, last = tile == 0, tile == 1
                        ins = pe.matmul(ps_o[0:T, P * slot:P * slot + P], pT[0:hi - lo, seq % 2, k, 0:T], values, start=first, stop=last)
                    return ins

                turn(0)
                for g in range(len(groups)):
                    if g + 1 < len(groups):
                        turn(g + 1)
                    ins = multiply(g)
                ins.then_inc(pv_done, 1)

            def rows_turned(b):
                pe.wait_ge(rows_ready, 3 * b.n + 3)
                for g, pieces in enumerate(((0, 1, 2, 3), (4, 5))):
                    turn_group(group_index(b, 9, g), [(rows[0:b.T, P * c:P * c + P], P) for c in pieces], b.T)

            pe.wait_ge(keys_loaded, 16 * KEY_LOADS)
            for b in BLOCKS[0:2]:
                for part in range(NHEADS):
                    index_pieces(b, portion(b, part))
            head_logits(BLOCKS[0], 0)
            for b, h, after in slots():
                other = ahead(b, 2)
                if after:
                    head_logits(*after, other, portion(other, h) if other else range(0))
                if h == 0 and b.n:
                    rows_turned(BLOCKS[b.n - 1])
                head_values(b, h)
            rows_turned(BLOCKS[NB])

        @block.scalar
        def _(act):
            def index_relu(b, part):
                T = b.T
                for piece in portion(b, part):
                    i, s = IH * segs_before[b.n] + piece, piece // IH
                    lo, hi = b.segs[s]
                    act.wait_ge(raw_scores, i + 1)
                    act.activation(relu[0:T, i % 3, 0:hi - lo], ps_i[0:T, i % 2, 0:hi - lo], ACT.Relu).then_inc(relu_ready, 1)
                    if piece % IH == IH - 1:
                        act.wait_ge(seg_summed, segs_before[b.n] + s + 1)
                        if s == 0 and b.n >= 2:
                            act.wait_ge(scores_taken, b.n - 1)
                        act.activation(scores[0:T, b.n % 2, lo:hi], ps_s[0:T, 0:hi - lo], ACT.Copy).then_inc(seg_kept, 1)

            def exponentials(b, h):
                u, T = b.n % 2, b.T
                act.wait_ge(neg_ready, NHEADS * b.n + h + 1)
                seq = NHEADS * b.n + h
                if h < NH:
                    row = probs[0:T, seq % 2, 0:b.S]
                    act.activation(row, row, ACT.Exp, bias=neg[0:T, u, h:h + 1], accum_out=sums[0:T, u, h:h + 1]).then_inc(exp_done, 1)
                    return
                act.wait_ge(turned, last_group(seq - 2) + 1)
                for mh in range(MH):
                    ins = act.activation(probs[0:T, seq % 2, 256 * mh:256 * mh + 256], ps_l[0:T, mh // 2, 256 * (mh % 2):256 * (mh % 2) + 256],
                                         ACT.Exp, bias=neg[0:T, u, 8 + mh:9 + mh], accum_out=sums[0:T, u, 8 + mh:9 + mh])
                ins.then_inc(exp_done, 1)

            for b in BLOCKS[0:2]:
                for part in range(NHEADS):
                    index_relu(b, part)
            exponentials(BLOCKS[0], 0)
            for b, h, after in slots():
                if ahead(b, 2):
                    index_relu(ahead(b, 2), h)
                if h == 0 and b.n:
                    copy_groups(act, BLOCKS[b.n - 1], 9)
                copy_groups(act, b, h)
                if after:
                    exponentials(*after)
            copy_groups(act, BLOCKS[NB], 9)

        @block.vector
        def _(dve):
            st = Steps(dve, dve_steps)

            def pick(b, part):
                T, S = b.T, b.S
                row, at, low_work = scores[0:T, b.n % 2, 0:S], mask[0:T, b.n % 2, 0:S], work[0:T, 0:S]
                col = lambda x, i=0: x[0:T, i:i + 1]
                if part == 0:
                    dve.wait_ge(seg_kept, segs_before[b.n + 1])
                if not b.keep:
                    if part == 0:
                        st.step(dve.memset(at, 0.0))
                        dve.memset(mask[0:CHUNK, b.n % 2, S - CHUNK:S], MASKED).then_inc(scores_taken, 1)
                        dve.wait_ge(scores_taken, b.n + 1)
                    return
                if part == 0:
                    dve.memset(failed[:, :], 0.0)
                    dve.memset(col(counts), 0.0)
                    dve.tensor_reduce(col(low), row, AX.X, ALU.min)
                    st.step(dve.tensor_reduce(col(mids), row, AX.X, ALU.max))
                    if not b.sample:
                        dve.memset(scores[0:CHUNK, b.n % 2, S - CHUNK:S], UNSEEN)
                    st.step(dve.tensor_tensor(col(spread), col(mids), col(low), ALU.subtract))
                    st.step(dve.tensor_scalar(steps[0:T, :], halves[0:T, :], col(spread), None, ALU.mult))
                    st.step(dve.tensor_tensor(col(mids, 1), col(mids), col(steps), ALU.subtract))
                elif part <= HALVINGS:
                    r = part
                    st.step(dve.tensor_scalar(low_work, row, col(mids, r), None, ALU.is_gt, ALU.add, accum_out=col(counts, r)))
                    if r < HALVINGS:
                        st.step(dve.tensor_scalar(col(back), col(counts, r), b.keep - 0.5, col(steps, r - 1), ALU.is_ge, ALU.mult))
                        st.step(dve.scalar_tensor_tensor(col(mids, r + 1), col(back), col(steps, r), col(mids, r), ALU.subtract, ALU.add))
                elif part == HALVINGS + 1:
                    st.step(dve.tensor_scalar(far[0:T, :], counts[0:T, :], b.keep - 0.5, FAR, ALU.is_ge, ALU.mult))
                    dve.tensor_tensor(mids[0:T, :], mids[0:T, :], far[0:T, :], ALU.add)
                    st.step(dve.tensor_tensor(counts[0:T, :], counts[0:T, :], far[0:T, :], ALU.subtract))
                    dve.tensor_reduce(col(above), counts[0:T, :], AX.X, ALU.max)
                    st.step(dve.tensor_reduce(col(bound), mids[0:T, :], AX.X, ALU.min))
                    st.step(dve.tensor_scalar(low_work, row, col(bound), -FAR, ALU.is_gt, ALU.mult))
                elif part == HALVINGS + 2:
                    st.step(dve.tensor_tensor(low_work, low_work, row, ALU.add))
                    st.step(dve.max(top[0:T, :], low_work))
                    st.step(dve.tensor_scalar(col(place), col(above), -1.0, b.keep - 1.0, ALU.mult, ALU.add))
                    st.step(dve.scalar_tensor_tensor(far[0:T, 0:8], places[0:T, 0:8], col(place), top[0:T, :], ALU.is_equal, ALU.mult))
                    st.step(dve.tensor_reduce(col(kth), far[0:T, 0:8], AX.X, ALU.add))
                else:
                    st.step(dve.tensor_scalar(at, row, col(kth), MASKED, ALU.is_lt, ALU.mult))
                    st.step(dve.tensor_scalar(far[0:T, 0:8], top[0:T, :], col(kth), None, ALU.is_ge))
                    st.step(dve.tensor_reduce(col(reached), far[0:T, 0:8], AX.X, ALU.add))
                    dve.tensor_scalar(col(crowded), col(reached), 8.0, None, ALU.is_ge)
                    st.step(dve.tensor_scalar(col(split_tie), col(reached), col(place), 1.0, ALU.subtract, ALU.not_equal))
                    st.step(dve.tensor_tensor(col(failed), col(crowded), col(split_tie), ALU.add))
                    with dve.If(failed_rows(st) > 0):
                        break_ties(b)
                    dve.memset(idle[:, :], 0.0).then_inc(scores_taken, 1)
                    dve.wait_ge(scores_taken, b.n + 1)

            def failed_rows(steps_of):
                steps_of.step(dve.transpose(failedT[:, :], failed[:, :]))
                with nc.allow_low_precision(reason="counts of rows"):
                    steps_of.step(dve.tensor_reduce(failures[:, :], failedT[:, :], AX.X, ALU.add))
                parts = [dve.value_load(failures[q:q + 1, 0:1], min_val=0, max_val=64) for q in range(0, P, 32)]
                return dve.snap(parts[0] + parts[1] + parts[2] + parts[3])

            def break_ties(b):
                T, S = b.T, b.S
                row, at, order = scores[0:T, b.n % 2, 0:S], mask[0:T, b.n % 2, 0:S], work[0:T, 0:S]
                col = lambda x, i=0: x[0:T, i:i + 1]
                own = Steps(dve, tie_steps)
                own.step(dve.tensor_scalar(col(place), col(place), 7.0, None, ALU.min))
                own.step(dve.scalar_tensor_tensor(chosen[0:T, 0:8], places[0:T, 0:8], col(place), top[0:T, :], ALU.is_equal, ALU.mult))
                own.step(dve.tensor_reduce(col(kth), chosen[0:T, 0:8], AX.X, ALU.add))
                own.step(dve.tensor_scalar(chosen[0:T, 0:8], top[0:T, :], col(kth), None, ALU.is_gt))
                own.step(dve.tensor_reduce(col(reached), chosen[0:T, 0:8], AX.X, ALU.add))
                own.step(dve.tensor_tensor(col(missing), col(reached), col(above), ALU.add))
                own.step(dve.tensor_scalar(col(missing), col(missing), -1.0, b.keep - 1.0, ALU.mult, ALU.add))
                own.step(dve.scalar_tensor_tensor(order, row, col(kth), falling[0:T, 0:S], ALU.is_equal, ALU.mult))
                own.step(dve.max(lowest[0:T, 0:8], order))
                own.step(dve.match_replace(at, lowest[0:T, 0:8], order, 0.0))
                own.step(dve.max(lowest[0:T, 8:16], at))
                own.step(dve.scalar_tensor_tensor(chosen[0:T, :], places[0:T, :], col(missing), lowest[0:T, :], ALU.is_equal, ALU.mult))
                own.step(dve.tensor_reduce(col(last_tie), chosen[0:T, :], AX.X, ALU.add))
                own.step(dve.tensor_scalar(at, order, col(last_tie), MASKED, ALU.is_lt, ALU.mult))
                own.step(dve.scalar_tensor_tensor(at, row, col(kth), at, ALU.is_le, ALU.mult))
                own.step(dve.tensor_scalar(col(failed), col(last_tie), 0.5, None, ALU.is_lt))
                total = failed_rows(own)
                dve.sem_clear(tie_steps)
                with dve.If(total > 0):
                    take_largest(b)

            def take_largest(b):
                T = b.T
                row, at, cur = scores[0:T, b.n % 2, 0:b.S], mask[0:T, b.n % 2, 0:b.S], work[0:T, 0:b.S]
                own = Steps(dve, general_steps)
                own.step(dve.max(top[0:T, :], row))
                own.step(dve.match_replace(cur, top[0:T, :], row, TAKEN))
                rounds = b.keep // 8 - 1
                with dve.Fori(0, rounds) as i:
                    own.done = 2 + 2 * i
                    own.step(dve.max(top[0:T, :], cur))
                    dve.memset(idle[:, :], 0.0)
                    own.step(dve.match_replace(cur, top[0:T, :], cur, TAKEN))
                own.done = 2 + 2 * rounds
                own.step(dve.tensor_scalar(at, cur, TAKEN_BELOW, MASKED, ALU.is_ge, ALU.mult))
                dve.sem_clear(general_steps)

            def mask_logits(b, h):
                u, T = b.n % 2, b.T
                first = logit_count(b, h, 0)
                if h == NH:
                    dve.wait_ge(logits, first + 1)
                    for half in range(2):
                        ins = dve.tensor_reduce(neg[0:T, u, 8 + 2 * half:10 + 2 * half], ps_l[0:T, half, :].rearrange("p (h n) -> p h n", n=MT), AX.X, ALU.max)
                    ins.then_inc(masked, 1)
                    dve.wait_ge(masked, first + 1)
                    dve.tensor_scalar(neg[0:T, u, 8:12], neg[0:T, u, 8:12], -1.0, None, ALU.mult).then_inc(neg_ready, 1)
                    return
                seq = NHEADS * b.n + h
                if seq >= 2:
                    dve.wait_ge(turned, last_group(seq - 2) + 1)
                for s, (lo, hi) in enumerate(b.segs):
                    dve.wait_ge(logits, first + s + 1)
                    dve.tensor_tensor_reduce(probs[0:T, seq % 2, lo:hi], ps_l[0:T, (first + s) % 2, 0:hi - lo], mask[0:T, u, lo:hi],
                                             1.0, -3.0e38, ALU.add, ALU.max, peaks[0:T, seq % 2, s:s + 1]).then_inc(masked, 1)
                dve.wait_ge(masked, first + len(b.segs))
                st.step(dve.tensor_reduce(neg[0:T, u, h:h + 1], peaks[0:T, seq % 2, 0:len(b.segs)], AX.X, ALU.max))
                dve.tensor_scalar(neg[0:T, u, h:h + 1], neg[0:T, u, h:h + 1], -1.0, None, ALU.mult).then_inc(neg_ready, 1)

            def divide(b, q):
                u, T = b.n % 2, b.T
                dve.wait_ge(pv_done, NHEADS * b.n + (GQ * (q + 1) if q < 2 else NHEADS))
                if q == 0 and b.n:
                    dve.wait_ge(turned, groups_before[b.n])
                st.step(dve.reciprocal(inv[0:T, u, 4 * q:4 * q + 4], sums[0:T, u, 4 * q:4 * q + 4]))
                src = ps_o[0:T, :].rearrange("p (h d) -> p h d", d=P)
                dst = rows[0:T, 256 * q:256 * q + 256].rearrange("p (h d) -> p h d", d=HD)
                scale = inv[0:T, u, 4 * q:4 * q + 4].unsqueeze(2).broadcast_to([T, 4, HD])
                if q < 2:
                    dve.tensor_tensor(dst, src[:, :, HD * q:HD * q + HD], scale, ALU.mult).then_inc(rows_ready, 1)
                    return
                for mh in range(MH):
                    o = HD * (mh % 2)
                    ins = dve.tensor_tensor(dst[:, mh], src[:, mh, o:o + HD], scale[:, mh], ALU.mult)
                ins.then_inc(rows_ready, 1)

            pick(BLOCKS[0], 0)
            mask_logits(BLOCKS[0], 0)
            for b, h, after in slots():
                if after:
                    mask_logits(*after)
                if h == 0 and b.n:
                    divide(BLOCKS[b.n - 1], 2)
                if h in (4, 8):
                    divide(b, h // GQ - 1)
                if h < 8 and not b.sample:
                    pick(ahead(b, 1), 2 * h)
                    pick(ahead(b, 1), 2 * h + 1)
            divide(BLOCKS[NB], 2)


HALF = ROWS // 2
NS, SUB = 3, HALF // 3
PROMPT_1 = SEQ - HALF
EDGES = [(a, min(a + P, HALF)) for a in range(0, HALF, P)]


def first(i):
    return isinstance(i, int) and i == 0


def iterations(eng, body, count, steps=None):
    start = steps.done if steps else 0
    body(0)
    per = steps.done - start if steps else 0
    with eng.Fori(1, count) as i:
        if steps:
            steps.done = start + i * per
        body(i)
    if steps:
        steps.done = start + count * per


def row_tiles(ch, starts):
    tiles = []
    cuts = sorted(set(starts) | ({PROMPT_1} if ch else set()) | {HALF})
    for lo, hi in zip(cuts[:-1], cuts[1:]):
        for a in range(lo, hi, P):
            w = min(P, hi - a)
            sample = ch == 1 and a >= PROMPT_1
            tiles.append((a, w, "sample" if sample else "prompt", a - PROMPT_1 if sample else HALF * ch + a))
    return tiles


def phase_mix(nc, t, ch, ident, ones, hT, nhi, nlo):
    with ExitStack() as ctx:
        m = Pool_(nc, ctx, f"mix{ch}")
        wraw = m.sb("wraw", [P, 2, KC, P])
        whi, wlo = m.sb("whi", [P, 2, KC, P], F32R), m.sb("wlo", [P, 2, KC, P], F32R)
        tiles = row_tiles(ch, [SUB * s for s in range(NS)])
        xs = m.sb("xs", [P, 2, len(tiles), P])
        sq, acc = m.sb("sq", [P, 2, HALF]), m.sb("acc", [P, HALF])
        gain = m.sb("gain", [P, KC])
        ss, rs, tmp = m.sb("ss", [P, len(EDGES)]), m.sb("rs", [P, len(EDGES)]), m.sb("tmp", [P, len(EDGES)])
        diag = m.sb("diag", [P, len(EDGES), P])
        ps_h, ps_n = m.ps("ps_h", [P, 2, NS, 512]), m.ps("ps_n", [P, 512])
        pair = lambda name: [m.sem(f"{name}{u}") for u in range(2)]
        mixed, mix_hi, mix_lo, gain_loaded = m.sem("mixed"), m.sem("mix_hi"), m.sem("mix_lo"), m.sem("gain_loaded")
        w_loaded, x_loaded, w_lo, product, kept, added = (pair(n) for n in ("w_loaded", "x_loaded", "w_lo", "product", "kept", "added"))
        summed, scaled, spread, normed, n_hi = (m.sem(n) for n in ("summed", "scaled", "spread", "normed", "n_hi"))
        pool_steps, dve_steps = m.sem("pool"), m.sem("dve")
        block = ctx.enter_context(nc.Block())

        @block.sync
        def _(sp):
            for k in range(KC):
                sp.dma_start(nlo[:, k, :].bitcast(F32), t["mixT"][P * k:P * k + P, HALF * ch:HALF * ch + HALF]).then_inc(mixed, 16)
            sp.dma_start(gain[:, :], t["norm2"].rearrange("l (c p) -> p (l c)", p=P), allow_slow_non_contiguous=True).then_inc(gain_loaded, 16)
            def load(i):
                for u in range(2):
                    cols = bass.ds((2 * i + u) * P, P)
                    if not first(i):
                        sp.wait_ge(w_lo[u], i)
                    sp.dma_start(wraw[:, u, :, :], t["w_out"].rearrange("l (c p) n -> p (l c) n", p=P)[:, :, cols]).then_inc(w_loaded[u], 16)
                    if not first(i):
                        sp.wait_ge(product[u], i)
                    for r, (_, w, kind, row) in enumerate(tiles):
                        sp.dma_start(xs[0:w, u, r, :], t[f"x_{kind}"][0, row:row + w, cols]).then_inc(x_loaded[u], 16)

            iterations(sp, load, KC // 2)

        @block.gpsimd
        def _(pool):
            def split(i):
                for u in range(2):
                    pool.wait_ge(w_loaded[u], 16 * (i + 1))
                    if not first(i):
                        pool.wait_ge(product[u], i)
                    one = ones[:, 0:1].unsqueeze(1).broadcast_to([P, KC, P])
                    pool.tensor_tensor(whi[:, u, :, :], wraw[:, u, :, :], one, ALU.mult).then_inc(pool_steps, 1)
                    pool.wait_ge(pool_steps, 2 * i + u + 1)
                    pool.tensor_tensor(wlo[:, u, :, :], wraw[:, u, :, :], whi[:, u, :, :].bitcast(F32), ALU.subtract).then_inc(w_lo[u], 1)

            iterations(pool, split, KC // 2)

        @block.tensor
        def _(pe):
            def columns(i):
                for u in range(2):
                    pe.wait_ge(w_lo[u], i + 1)
                    if not first(i):
                        pe.wait_ge(kept[u], i)
                    for k in range(KC):
                        pe.wait_ge(mix_lo, k + 1)
                        for n, (a, b) in enumerate(((whi, nhi), (whi, nlo), (wlo, nhi))):
                            for s in range(NS):
                                pe.matmul(ps_h[:, u, s, 0:SUB], a[:, u, k, :], b[:, k, SUB * s:SUB * s + SUB], start=(k == 0 and n == 0), stop=False)
                    pe.wait_ge(x_loaded[u], 16 * len(tiles) * (i + 1))
                    for r, (col, w, _, _) in enumerate(tiles):
                        s, o = col // SUB, col % SUB
                        ins = pe.matmul(ps_h[:, u, s, o:o + w], xs[0:w, u, r, :], ident[0:w, 0:w], start=False, stop=(o + w == SUB))
                    ins.then_inc(product[u], 1)

            iterations(pe, columns, KC // 2)
            for u in range(2):
                pe.wait_ge(added[u], KC // 2)
            for j, (lo, hi) in enumerate(EDGES):
                ins = pe.matmul(ps_n[0:hi - lo, j:j + 1], acc[:, lo:hi], ones[:, 0:1], start=True, stop=True)
            ins.then_inc(summed, 1)
            pe.wait_ge(scaled, 1)
            wide = ps_h[:, 0, :, :].rearrange("p s n -> p (s n)")
            for j, (lo, hi) in enumerate(EDGES):
                ins = pe.matmul(wide[:, lo:hi], ones[0:hi - lo, :], diag[0:hi - lo, j, 0:hi - lo], start=True, stop=True)
            ins.then_inc(spread, 1)

        @block.scalar
        def _(act):
            for k in range(KC):
                act.wait_ge(mixed, 16 * KC)
                act.activation(nhi[:, k, :], nlo[:, k, :].bitcast(F32), ACT.Copy).then_inc(mix_hi, 1)

            def keep(i):
                for u in range(2):
                    act.wait_ge(product[u], i + 1)
                    if not first(i):
                        act.wait_ge(added[u], i)
                    src = ps_h[:, u, :, 0:SUB]
                    act.activation(sq[:, u, :].rearrange("p (s n) -> p s n", s=NS), src, ACT.Square)
                    act.activation(hT[:, bass.ds(2 * i + u, 1), :].rearrange("p c (s n) -> p (c s) n", s=NS), src, ACT.Copy).then_inc(kept[u], 1)

            iterations(act, keep, KC // 2)
            for c in range(KC):
                act.wait_ge(normed, c + 1)
                act.activation(nhi[:, c, :], sq[:, c % 2, :], ACT.Copy).then_inc(n_hi, 1)

        @block.vector
        def _(dve):
            st = Steps(dve, dve_steps)
            st.step(dve.memset(acc[:, :], 0.0))
            st.step(dve.memset(ss[:, :], 1.0))
            for k in range(KC):
                dve.wait_ge(mix_hi, k + 1)
                dve.tensor_tensor(nlo[:, k, :], nlo[:, k, :].bitcast(F32), nhi[:, k, :].bitcast(F32), ALU.subtract).then_inc(mix_lo, 1)
            def add(i):
                for u in range(2):
                    dve.wait_ge(kept[u], i + 1)
                    if u:
                        dve.wait_ge(added[0], i + 1)
                    elif not first(i):
                        dve.wait_ge(added[1], i)
                    dve.tensor_tensor(acc[:, :], acc[:, :], sq[:, u, :], ALU.add).then_inc(added[u], 1)

            iterations(dve, add, KC // 2)
            full = HALF // P
            dve.wait_ge(summed, 1)
            dve.tensor_scalar(ss[:, 0:full], ps_n[:, 0:full], 1.0 / D, EPS, ALU.mult, ALU.add)
            rest = HALF - P * full
            st.step(dve.tensor_scalar(ss[0:rest, full:full + 1], ps_n[0:rest, full:full + 1], 1.0 / D, EPS, ALU.mult, ALU.add))
            rsqrt(dve, st, rs[:, :], ss[:, :], tmp[:, :])
            for j in range(len(EDGES)):
                ins = dve.tensor_scalar(diag[:, j, :], ident[:, :], rs[:, j:j + 1], None, ALU.mult)
            ins.then_inc(scaled, 1)
            dve.wait_ge(spread, 1)
            dve.wait_ge(gain_loaded, 16)
            wide = ps_h[:, 0, :, :].rearrange("p s n -> p (s n)")[:, 0:HALF]

            def low(c):
                dve.wait_ge(n_hi, c + 1)
                dve.tensor_tensor(nlo[:, c, :], sq[:, c % 2, :], nhi[:, c, :].bitcast(F32), ALU.subtract).then_inc(mix_lo, 1)
                dve.wait_ge(mix_lo, KC + c + 1)

            for c in range(KC):
                dve.scalar_tensor_tensor(sq[:, c % 2, :], hT[:, c, :], gain[:, c:c + 1], wide, ALU.mult, ALU.mult).then_inc(normed, 1)
                dve.wait_ge(normed, c + 1)
                if c:
                    low(c - 1)
            low(KC - 1)


def phase_feed(nc, t, ch, ident, ones, hT, nhi, nlo, conv, hist):
    with ExitStack() as ctx:
        m = Pool_(nc, ctx, f"ffn{ch}")
        raw_up, raw_down = m.sb("raw_up", [P, 2, KC, 2 * P]), m.sb("raw_down", [P, 2, D])
        up_hi, up_lo = m.sb("up_hi", [P, 4, KC, P], F32R), m.sb("up_lo", [P, 4, KC, P], F32R)
        down_hi, down_lo = m.sb("down_hi", [P, 2, D], F32R), m.sb("down_lo", [P, 2, D], F32R)
        a_hi, a_lo = m.sb("a_hi", [P, 2, HALF], F32R), m.sb("a_lo", [P, 2, HALF], F32R)
        up = m.sb("up", [P, HALF + 4])
        gv = m.sb("gv", [P, 2, HALF])
        idle = m.sb("idle", [P, 2])
        taps = m.sb("taps", [P, 8, 2])
        ps_u, ps_d = m.ps("ps_u", [P, 2, NS, 512]), m.ps("ps_d", [P, 2, 512])
        raw_loaded, down_loaded = [m.sem("raw_loaded0"), m.sem("raw_loaded1")], m.sem("down_loaded")
        up_ready, down_ready, unit_done, based = m.sem("up_ready"), m.sem("down_ready"), m.sem("unit_done"), m.sem("based")
        tap_ready, convolved, gated, a_full, a_high, a_ready = (m.sem(n) for n in ("tap_ready", "convolved", "gated", "a_full", "a_high", "a_ready"))
        partial, partial_read = [m.sem("partial0"), m.sem("partial1")], [m.sem("partial_read0"), m.sem("partial_read1")]
        pool_steps, dve_steps, hist_moved = m.sem("pool"), m.sem("dve"), m.sem("hist_moved")
        y_turned, y_kept, stored = m.sem("y_turned"), m.sem("y_kept"), [m.sem("stored0"), m.sem("stored1")]
        NIT = FT // 2
        runs = [(0, HALF, 2)] if ch == 0 else [(0, PROMPT_1, 2), (PROMPT_1, HALF, 4)]
        out_tiles = row_tiles(ch, [0])

        block = ctx.enter_context(nc.Block())

        @block.sync
        def _(sp):
            def load(it):
                for half in range(2):
                    if not first(it):
                        sp.wait_ge(up_ready, 4 * it - 1 + half)
                    src = t["w_up"].rearrange("l (c p) (h n) -> p (l h) c n", p=P, h=2)[:, half, :, bass.ds(it * (2 * P), 2 * P)]
                    sp.dma_start(raw_up[:, half, :, :], src).then_inc(raw_loaded[half], 16)
                if not first(it):
                    sp.wait_ge(down_ready, it)
                sp.dma_start(raw_down[:, :, :], t["w_down"].rearrange("l (f p) d -> p (l f) d", p=P)[:, bass.ds(it * 2, 2), :]).then_inc(down_loaded, 16)

            iterations(sp, load, NIT)
            for i, (_, w, kind, row) in enumerate(out_tiles):
                sp.wait_ge(y_kept, i + 1)
                sp.dma_start(t[f"y_{kind}"][0, row:row + w, :], gv[0:w, i % 2, 0:D]).then_inc(stored[i % 2], 16)
            sp.wait_ge(stored[0], 16 * ((len(out_tiles) + 1) // 2))
            sp.wait_ge(stored[1], 16 * (len(out_tiles) // 2))

        @block.gpsimd
        def _(pool):
            st = Steps(pool, pool_steps)

            def split(hi, lo, raw, ready):
                st.step(pool.tensor_tensor(hi, raw, ones[:, 0:1].unsqueeze(1).broadcast_to(list(raw.shape)), ALU.mult))
                pool.tensor_tensor(lo, raw, hi.bitcast(F32), ALU.subtract).then_inc(ready, 1)

            def body(it):
                for q in range(4):
                    e, half = q // 2, q % 2
                    pool.wait_ge(raw_loaded[half], 16 * (it + 1))
                    if not first(it):
                        pool.wait_ge(unit_done, 4 * it - 3 + q)
                    split(up_hi[:, q], up_lo[:, q], raw_up[:, half, :, P * e:P * e + P], up_ready)
                pool.wait_ge(down_loaded, 16 * (it + 1))
                if not first(it):
                    for u in range(2):
                        pool.wait_ge(partial[u], it * (KC * NS // 2))
                split(down_hi[:, :, :], down_lo[:, :, :], raw_down[:, :, :], down_ready)

            iterations(pool, body, NIT, steps=st)

        @block.tensor
        def _(pe):
            def unit(it, q):
                half = q % 2
                pe.wait_ge(up_ready, 4 * it + q + 1)
                if not (first(it) and q < 2):
                    pe.wait_ge(based, 4 * it + q - 1)
                for k in range(KC):
                    for n, (a, b) in enumerate(((up_hi, nhi), (up_hi, nlo), (up_lo, nhi))):
                        for s in range(NS):
                            ins = pe.matmul(ps_u[:, half, s, 0:SUB], a[:, q, k, :], b[:, k, SUB * s:SUB * s + SUB],
                                            start=(k == 0 and n == 0), stop=(k == KC - 1 and n == 2))
                ins.then_inc(unit_done, 1)

            def down(it):
                pe.wait_ge(a_ready, 2 * it + 2)
                pe.wait_ge(down_ready, it + 1)
                for j in range(KC * NS):
                    c, s = j // NS, j % NS
                    pe.wait_ge(partial_read[j % 2], it * (KC * NS // 2) + (j // 2 + 1))
                    for e in range(2):
                        for n, (a, b) in enumerate(((down_hi, a_hi), (down_hi, a_lo), (down_lo, a_hi))):
                            ins = pe.matmul(ps_d[:, j % 2, 0:SUB], a[:, e, P * c:P * c + P], b[:, e, SUB * s:SUB * s + SUB],
                                            start=(e == 0 and n == 0), stop=(e == 1 and n == 2))
                    ins.then_inc(partial[j % 2], 1)

            for q in range(4):
                unit(0, q)
            with pe.Fori(1, NIT) as it:
                unit(it, 0)
                down(it - 1)
                for q in range(1, 4):
                    unit(it, q)
            down(NIT - 1)
            for u in range(2):
                pe.wait_ge(partial_read[u], NIT * KC * NS // 2 + 1)
            pe.wait_ge(based, 4 * NIT)
            for i, (col, w, _, _) in enumerate(out_tiles):
                if i >= 2:
                    pe.wait_ge(y_kept, i - 1)
                for c in range(KC):
                    ins = pe.transpose(ps_u[0:w, i % 2, c // 4, P * (c % 4):P * (c % 4) + P], hT[:, c, col:col + w], ident[:, :])
                ins.then_inc(y_turned, 1)

        @block.scalar
        def _(act):
            def body(it):
                act.wait_ge(tap_ready, it + 1)
                for q in range(4):
                    e, half = q // 2, q % 2
                    act.wait_ge(unit_done, 4 * it + q + 1)
                    if not (first(it) and q == 0):
                        act.wait_ge(convolved, 4 * it + q)
                    for lo, hi, shift in runs:
                        whole = hi // SUB if lo == 0 else 0
                        if whole:
                            act.activation(up[:, shift:shift + whole * SUB].rearrange("p (s n) -> p s n", n=SUB), ps_u[:, half, 0:whole, 0:SUB], ACT.Copy)
                        a = max(lo, whole * SUB)
                        if a < hi:
                            act.activation(up[:, a + shift:hi + shift], ps_u[:, half, a // SUB, a % SUB:(hi - 1) % SUB + 1], ACT.Copy)
                    if not (first(it) and q < 2):
                        act.wait_ge(a_ready, 2 * it + e)
                    act.activation(gv[:, half, :].rearrange("p (s n) -> p s n", s=NS), ps_u[:, half, :, 0:SUB], ACT.Identity,
                                   scale=taps[:, 4 + half, e:e + 1], bias=taps[:, 6 + half, e:e + 1]).then_inc(based, 1)
                    act.wait_ge(convolved, 4 * it + q + 1)
                    if half == 0:
                        act.activation(gv[:, 0, :], gv[:, 0, :], ACT.Silu).then_inc(gated, 1)
                    else:
                        act.wait_ge(a_full, 2 * it + e + 1)
                        act.activation(a_hi[:, e, :], gv[:, 1, :], ACT.Copy).then_inc(a_high, 1)

            iterations(act, body, NIT)
            for i, (_, w, _, _) in enumerate(out_tiles):
                act.wait_ge(y_turned, i + 1)
                if i >= 2:
                    act.wait_ge(stored[i % 2], 16 * (i // 2))
                act.activation(gv[0:w, i % 2, 0:D].rearrange("p (s n) -> p s n", s=2), ps_u[0:w, i % 2, 0:2, :], ACT.Copy).then_inc(y_kept, 1)

        @block.vector
        def _(dve):
            st = Steps(dve, dve_steps)
            tails = [(0, HALF + 2)] if ch == 0 else [(0, PROMPT_1 + 2), (1, HALF + 4)]

            def hist_at(which, it, q):
                return hist[which][:, :, bass.ds(it * 2 + (FT * (q % 2) + q // 2), 1)].rearrange("p j f -> p (j f)")

            def body(it):
                dve.tensor_copy(taps[:, :, :], conv[:, :, bass.ds(it * 2, 2)]).then_inc(tap_ready, 1)
                dve.wait_ge(tap_ready, it + 1)
                for q in range(4):
                    e, half = q // 2, q % 2
                    if not (first(it) and q == 0):
                        dve.wait_ge(convolved, 4 * it + q)
                    for which, (lo, _, shift) in enumerate(runs):
                        dve.tensor_copy(up[:, lo + shift - 2:lo + shift], hist_at(which, it, q)).then_inc(hist_moved, 1)
                    dve.wait_ge(hist_moved, len(runs) * (4 * it + q + 1))
                    dve.wait_ge(based, 4 * it + q + 1)
                    for j in (1, 0):
                        for lo, hi, shift in runs:
                            ins = dve.scalar_tensor_tensor(gv[:, half, lo:hi], up[:, lo + shift + j - 2:hi + shift + j - 2], taps[:, 2 * j + half, e:e + 1],
                                                           gv[:, half, lo:hi], ALU.mult, ALU.add)
                            if j:
                                st.step(ins)
                    for which, end in tails:
                        ins = dve.tensor_copy(hist_at(which, it, q), up[:, end - 2:end])
                    ins.then_inc(convolved, 1)
                    if half:
                        dve.wait_ge(gated, 2 * it + e + 1)
                        dve.wait_ge(convolved, 4 * it + q + 1)
                        dve.tensor_tensor(gv[:, 1, :], gv[:, 0, :], gv[:, 1, :], ALU.mult).then_inc(a_full, 1)
                        dve.wait_ge(a_high, 2 * it + e + 1)
                        dve.tensor_tensor(a_lo[:, e, :], gv[:, 1, :], a_hi[:, e, :].bitcast(F32), ALU.subtract).then_inc(a_ready, 1)
                        dve.wait_ge(a_ready, 2 * it + e + 1)
                    if q == 0 and not first(it):
                        add(it - 1)

            def add(it):
                for j in range(KC * NS):
                    c, s = j // NS, j % NS
                    dve.wait_ge(partial[j % 2], it * (KC * NS // 2) + (j // 2 + 1))
                    at = hT[:, c, SUB * s:SUB * s + SUB]
                    dve.tensor_tensor(at, at, ps_d[:, j % 2, 0:SUB], ALU.add).then_inc(partial_read[j % 2], 1)

            for u in range(2):
                dve.memset(idle[:, u:u + 1], 0.0).then_inc(partial_read[u], 1)
            iterations(dve, body, NIT, steps=st)
            add(NIT - 1)


def load_conv(nc, t, ident, ones, conv, hist):
    with ExitStack() as ctx:
        m = Pool_(nc, ctx, "conv")
        FU = 2 * FT
        rows = m.sb("rows", [P, 2, P])
        before = m.sb("before", [2 * FU, P])
        ps = m.ps("ps", [P, 3, 512])
        loaded, turned, done = m.sem("loaded"), m.sem("turned"), m.sem("done")
        block = ctx.enter_context(nc.Block())
        src_w = t["conv_w"].rearrange("l j (f p) -> (l j f) p", p=P)
        src_b = t["conv_b"].rearrange("l (f p) -> (l f) p", p=P)

        @block.sync
        def _(sp):
            sp.dma_start(rows[0:2 * FU, 0, :], src_w[0:2 * FU]).then_inc(loaded, 16)
            sp.dma_start(rows[0:FU, 1, :], src_w[2 * FU:3 * FU]).then_inc(loaded, 16)
            sp.dma_start(rows[FU:2 * FU, 1, :], src_b).then_inc(loaded, 16)
            sp.dma_start(before[:, :], t["state_ffn_conv"].rearrange("l b j (f p) -> (l b j f) p", p=P)).then_inc(loaded, 16)

        @block.tensor
        def _(pe):
            pe.wait_ge(loaded, 64)
            for n in range(3):
                src = before[:, :] if n == 2 else rows[0:2 * FU, n, :]
                pe.transpose(ps[:, n, 0:2 * FU], src, ident[0:2 * FU, 0:2 * FU]).then_inc(turned, 1)

        @block.vector
        def _(dve):
            dve.wait_ge(turned, 3)
            for n in range(2):
                dve.tensor_copy(conv[:, 4 * n:4 * n + 4, :].rearrange("p j f -> p (j f)"), ps[:, n, 0:2 * FU]).then_inc(done, 1)
            dve.tensor_copy(hist[1][:, :, :].rearrange("p j f -> p (j f)"), ps[:, 2, 0:2 * FU]).then_inc(done, 1)
            dve.memset(hist[0][:, :, :], 0.0).then_inc(done, 1)
            dve.memset(ones[:, :], 1.0).then_inc(done, 1)
            dve.wait_ge(done, 5)


def store_conv(nc, t, ident, hist):
    with ExitStack() as ctx:
        m = Pool_(nc, ctx, "tail")
        FU = 2 * FT
        rows = m.sb("rows", [2 * FU, 2, P])
        ps = m.ps("ps", [2 * FU, 2, 512])
        turned, kept, stored = m.sem("turned"), m.sem("kept"), m.sem("stored")
        block = ctx.enter_context(nc.Block())

        @block.tensor
        def _(pe):
            for n in range(2):
                pe.transpose(ps[:, n, 0:P], hist[n][:, :, :].rearrange("p j f -> p (j f)"), ident[:, :]).then_inc(turned, 1)

        @block.vector
        def _(dve):
            dve.wait_ge(turned, 2)
            dve.tensor_copy(rows[:, :, :], ps[:, :, 0:P]).then_inc(kept, 1)

        @block.sync
        def _(sp):
            sp.wait_ge(kept, 1)
            for n, kind in enumerate(("prompt", "sample")):
                sp.dma_start(t[f"new_conv_{kind}"].rearrange("l b j (f p) -> (l b j f) p", p=P), rows[:, n, :]).then_inc(stored, 16)
            sp.wait_ge(stored, 32)


OUTPUTS = (
    ("y_prompt", (1, SEQ, D)), ("y_sample", (1, TS, D)),
    ("new_k_prompt", (1, 1, SEQ, NKV, HD)), ("new_v_prompt", (1, 1, SEQ, NKV, HD)), ("new_kidx_prompt", (1, 1, SEQ, ID)),
    ("new_mem_k_prompt", (1, 1, MT, MH, HD)), ("new_mem_v_prompt", (1, 1, MT, MH, HD)),
    ("new_pool_prompt", (1, 1, HIST, PW)), ("new_conv_prompt", (1, 1, 2, 2 * FF)),
    ("new_k_sample", (1, 1, TS, NKV, HD)), ("new_v_sample", (1, 1, TS, NKV, HD)), ("new_kidx_sample", (1, 1, TS, ID)),
    ("new_pool_sample", (1, 1, HIST, PW)), ("new_conv_sample", (1, 1, 2, 2 * FF)),
)


def program(nc, t):
    t["sT"] = nc.dram_tensor("scratch_sT", (NB + 1, P, NSLOT * P), F32).ap()
    t["mixT"] = nc.dram_tensor("scratch_mixT", (D, ROWS), F32).ap()
    with ExitStack() as ctx:
        ident = ctx.enter_context(nc.sbuf_tensor("ident", [P, P], F32))
        with ExitStack() as attention:
            k = Pool_(nc, attention, "keep")
            keep = {
                "ident": ident,
                "ksT": k.sb("ksT", [P, NKV, LS], F32R), "kisT": k.sb("kisT", [P, LS], F32R),
                "vs": k.sb("vs", [P, 5, NKV * HD]),
                "mkT": k.sb("mkT", [P, 2, MH, MT], F32R),
                "mv": k.sb("mv", [P, 2, 2, MH * HD]),
                "w8": k.sb("w8", [P, NB + 1, IH]),
                "pool_scale": k.sb("pool_scale", [P, 2]),
            }
            phase_memory(nc, t, keep)
            phase_project(nc, t, keep)
            phase_attend(nc, t, keep)
        clear_semaphores(nc)
        f = Pool_(nc, ctx, "feed")
        hT = f.sb("hT", [P, KC, HALF])
        nhi, nlo = f.sb("nhi", [P, KC, HALF], F32R), f.sb("nlo", [P, KC, HALF], F32R)
        ones = f.sb("ones", [P, P])
        conv = f.sb("conv", [P, 8, FT])
        hist = [f.sb(f"hist{n}", [P, 2, 2 * FT]) for n in range(2)]
        load_conv(nc, t, ident, ones, conv, hist)
        for ch in range(2):
            phase_mix(nc, t, ch, ident, ones, hT, nhi, nlo)
            phase_feed(nc, t, ch, ident, ones, hT, nhi, nlo, conv, hist)
        store_conv(nc, t, ident, hist)


def constants():
    f = np.float32
    pos = np.arange(SEQ, dtype=f)[:, None]
    table = []
    for half in (8, 4):
        inv = np.power(f(500000.0), -np.arange(half, dtype=f) / f(half)).astype(f)
        ang = (pos * inv[None]).astype(f).astype(np.float64)
        cos, sin = np.cos(ang).astype(f), np.sin(ang).astype(f)
        table += [cos, cos, -sin, sin]
    s, r = np.arange(P)[:, None], np.arange(P)[None, :]
    band, first, old = [], [], []
    for w in WINDOWS:
        inside = (s <= r) & (s > r - w)
        band.append(inside / f(w) - (s == r))
        first.append(inside / np.minimum(w, r + 1).astype(f) - (s == r))
        old.append(((s - P) > r - w)[96:] / f(w))
    halves = np.broadcast_to(f(0.5) ** np.arange(1, HALVINGS + 1, dtype=f), (P, HALVINGS))
    places = np.broadcast_to(np.arange(16, dtype=f), (P, 16))
    return {"halves": halves.astype(f), "places": places.astype(f), "falling": np.arange(SEQ, 0, -1, dtype=f)[None], "rope_table": np.concatenate(table, 1).astype(f), "band": np.array(band, f), "band_first": np.array(first, f),
            "band_old": np.array(old, f)}


def kernel(**inputs):
    import concourse.bacc as bacc
    from concourse.bass_utils import run_bass_kernel_spmd

    nc = bacc.Bacc("TRN2", target_bir_lowering=False, num_devices=1)
    arrays, t = {}, {}
    for name, a in list(inputs.items()) + list(constants().items()):
        a = np.ascontiguousarray(a)
        arrays[f"in_{name}"] = a
        t[name] = nc.dram_tensor(f"in_{name}", a.shape, mybir.dt.from_np(a.dtype), kind="ExternalInput").ap()
    for name, shape in OUTPUTS:
        t[name] = nc.dram_tensor(f"out_{name}", shape, F32, kind="ExternalOutput").ap()
    program(nc, t)
    r = run_bass_kernel_spmd(nc, [arrays], core_ids=[0])
    return tuple(r.results[0][f"out_{name}"] for name, _ in OUTPUTS)
```
